# Optimizing a Trainium2 kernel written in Bass

```python
import math
import jax, jax.numpy as jnp
from jax import lax
import numpy as np

D_MODEL = 1024
BATCH = 1
SEQ = 512
DEPTH = 2

N_META = 16
D_MIX = D_MODEL
ATTN_WIDTH = D_MIX // 2
CONV_CH = D_MIX - ATTN_WIDTH
N_ATTN_HEADS = 4
V_HEAD_DIM = ATTN_WIDTH // N_ATTN_HEADS
HEAD_DIM = V_HEAD_DIM // 2
QK_WIDTH = N_ATTN_HEADS * 2 * HEAD_DIM
IN_WIDTH = 2 * QK_WIDTH + ATTN_WIDTH + 2 * CONV_CH
CONV_WIDTH = 31
D_FF = -(-8 * D_MODEL // (3 * 256)) * 256
ROPE_THETA = 10000.0
Q_BLOCK = 128
NORM_EPS = 1e-5


def rmsnorm(x, g):
    x32 = x.astype(jnp.float32)
    y = x32 * lax.rsqrt(jnp.mean(x32 * x32, axis=-1, keepdims=True) + NORM_EPS)
    return (y * g.astype(jnp.float32)).astype(x.dtype)

def layer_norm(x, g, b):
    x32 = x.astype(jnp.float32)
    mu = jnp.mean(x32, axis=-1, keepdims=True)
    xc = x32 - mu
    y = xc * lax.rsqrt(jnp.mean(xc * xc, axis=-1, keepdims=True) + NORM_EPS)
    return (y * g.astype(jnp.float32) + b.astype(jnp.float32)).astype(x.dtype)

def rope_tables(length, dtype):
    pos = jnp.arange(length, dtype=jnp.float32)
    inv = ROPE_THETA ** (-jnp.arange(0, HEAD_DIM, 2, dtype=jnp.float32) / HEAD_DIM)
    ang = pos[:, None] * inv[None, :]
    ang = jnp.concatenate([ang, ang], axis=-1)
    return jnp.cos(ang).astype(dtype), jnp.sin(ang).astype(dtype)

def apply_rope(t, cos, sin):
    c = cos[None, :, None, None, :]
    s = sin[None, :, None, None, :]
    t1, t2 = jnp.split(t, 2, axis=-1)
    return t * c + jnp.concatenate([-t2, t1], axis=-1) * s

def diff_attention(q, k, v, lam, sub_g, lam_init):
    B, L = q.shape[0], q.shape[1]
    n_blk = -(-L // Q_BLOCK)
    L_pad = n_blk * Q_BLOCK
    pad = L_pad - L
    q = jnp.pad(q, ((0, 0), (0, pad), (0, 0), (0, 0), (0, 0)))
    k = jnp.pad(k, ((0, 0), (0, pad), (0, 0), (0, 0), (0, 0)))
    v = jnp.pad(v, ((0, 0), (0, pad), (0, 0), (0, 0)))
    qb = q.reshape(B, n_blk, Q_BLOCK, N_ATTN_HEADS, 2, HEAD_DIM).transpose(1, 0, 2, 3, 4, 5)
    k_pos = jnp.arange(L_pad)
    scale = HEAD_DIM ** -0.5

    def one_block(args):
        q_blk, start = args
        s = jnp.einsum('bqhcd,bkhcd->bhcqk', q_blk, k).astype(jnp.float32) * scale
        q_pos = start + jnp.arange(Q_BLOCK)
        mask = k_pos[None, :] <= q_pos[:, None]
        s = jnp.where(mask, s, -jnp.inf)
        p = jax.nn.softmax(s, axis=-1)
        a = p[:, :, 0] - lam * p[:, :, 1]
        return jnp.einsum('bhqk,bkhe->bqhe', a.astype(v.dtype), v)

    starts = jnp.arange(n_blk) * Q_BLOCK
    o = lax.map(one_block, (qb, starts))
    o = o.transpose(1, 0, 2, 3, 4).reshape(B, L_pad, N_ATTN_HEADS, V_HEAD_DIM)[:, :L]
    o = rmsnorm(o, sub_g) * (1.0 - lam_init)
    return o.reshape(B, L, ATTN_WIDTH)

def conformer_conv(u, conv_w, conv_b, ln_g, ln_b):
    a, gate = jnp.split(u, 2, axis=-1)
    z = a * jax.nn.sigmoid(gate)
    z = lax.conv_general_dilated(
        z, conv_w[:, None, :], window_strides=(1,), padding=((CONV_WIDTH - 1, 0),),
        dimension_numbers=('NWC', 'WIO', 'NWC'), feature_group_count=CONV_CH)
    z = z + conv_b
    z = layer_norm(z, ln_g, ln_b)
    return jax.nn.silu(z)

def first_inputs(seed: int = 0) -> dict:
    key = jax.random.key(seed)
    ks = jax.random.split(key, 20)
    f = jnp.float32
    nrm = lambda k, shape, s: jax.random.normal(k, shape, f) * s
    return {
        "x": nrm(ks[0], (BATCH, SEQ, D_MODEL), 1.0),
        "meta_tokens": nrm(ks[1], (N_META, D_MODEL), 1.0),
        "norm1_g": 1.0 + nrm(ks[2], (DEPTH, D_MODEL), 0.02),
        "w_in": nrm(ks[3], (DEPTH, D_MODEL, IN_WIDTH), D_MODEL ** -0.5),
        "b_glu": nrm(ks[4], (DEPTH, 2 * CONV_CH), 0.02),
        "conv_w": nrm(ks[5], (DEPTH, CONV_WIDTH, CONV_CH), CONV_WIDTH ** -0.5),
        "conv_b": nrm(ks[6], (DEPTH, CONV_CH), 0.02),
        "conv_ln_g": 1.0 + nrm(ks[7], (DEPTH, CONV_CH), 0.02),
        "conv_ln_b": nrm(ks[8], (DEPTH, CONV_CH), 0.02),
        "lam_q1": nrm(ks[9], (DEPTH, HEAD_DIM), 0.1),
        "lam_k1": nrm(ks[10], (DEPTH, HEAD_DIM), 0.1),
        "lam_q2": nrm(ks[11], (DEPTH, HEAD_DIM), 0.1),
        "lam_k2": nrm(ks[12], (DEPTH, HEAD_DIM), 0.1),
        "subln_g": 1.0 + nrm(ks[13], (DEPTH, V_HEAD_DIM), 0.02),
        "w_out": nrm(ks[14], (DEPTH, D_MIX, D_MODEL), D_MIX ** -0.5),
        "norm2_g": 1.0 + nrm(ks[15], (DEPTH, D_MODEL), 0.02),
        "w_gate_up": nrm(ks[16], (DEPTH, D_MODEL, 2 * D_FF), D_MODEL ** -0.5),
        "w_down": nrm(ks[17], (DEPTH, D_FF, D_MODEL), D_FF ** -0.5),
        "final_g": 1.0 + nrm(ks[18], (D_MODEL,), 0.02),
    }

def first_block(x, meta_tokens, norm1_g, w_in, b_glu, conv_w, conv_b, conv_ln_g, conv_ln_b,
              lam_q1, lam_k1, lam_q2, lam_k2, subln_g, w_out, norm2_g, w_gate_up, w_down,
              final_g):
    B, S, D = x.shape
    meta = jnp.broadcast_to(meta_tokens[None].astype(x.dtype), (B, N_META, D))
    h = jnp.concatenate([meta, x], axis=1)
    L = S + N_META
    cos, sin = rope_tables(L, x.dtype)
    for l in range(DEPTH):
        lam_init = 0.8 - 0.6 * math.exp(-0.3 * l)
        hn = rmsnorm(h, norm1_g[l])
        proj = hn @ w_in[l]
        q, k, v, u = jnp.split(proj, [QK_WIDTH, 2 * QK_WIDTH, 2 * QK_WIDTH + ATTN_WIDTH], axis=-1)
        q = apply_rope(q.reshape(B, L, N_ATTN_HEADS, 2, HEAD_DIM), cos, sin)
        k = apply_rope(k.reshape(B, L, N_ATTN_HEADS, 2, HEAD_DIM), cos, sin)
        v = v.reshape(B, L, N_ATTN_HEADS, V_HEAD_DIM)
        lam = (jnp.exp(jnp.sum(lam_q1[l].astype(jnp.float32) * lam_k1[l].astype(jnp.float32)))
               - jnp.exp(jnp.sum(lam_q2[l].astype(jnp.float32) * lam_k2[l].astype(jnp.float32)))
               + lam_init)
        attn_out = diff_attention(q, k, v, lam, subln_g[l], lam_init)
        conv_out = conformer_conv(u + b_glu[l], conv_w[l], conv_b[l],
                                  conv_ln_g[l], conv_ln_b[l])
        h = h + jnp.concatenate([attn_out, conv_out], axis=-1) @ w_out[l]
        hn = rmsnorm(h, norm2_g[l])
        gate, up = jnp.split(hn @ w_gate_up[l], 2, axis=-1)
        h = h + (jax.nn.silu(gate) * up) @ w_down[l]
    h = rmsnorm(h, final_g)
    return h[:, N_META:]


CHUNK = 64
N_MIXERS = 2
ROPE_THETA_2 = 500000.0
EPS = 1e-6

A_HEADS = 16
A_KV_HEADS = 4
A_HEAD_DIM = 64
A_ROT = A_HEAD_DIM // 4
IDX_HEADS = 8
IDX_DIM = 64
IDX_ROT = IDX_DIM // 4
IDX_TOPK_MAX = 256
IDX_WEIGHT_SCALE = (IDX_HEADS ** -0.5) * (IDX_DIM ** -0.5)
A_QBLK = CHUNK
A_IN = A_HEADS * A_HEAD_DIM + 2 * A_KV_HEADS * A_HEAD_DIM + IDX_HEADS * IDX_DIM + IDX_DIM + IDX_HEADS

B_HEADS = 16
B_NOPE = 64
B_ROPE = 32
B_V = 64
B_Q_LORA = 384
B_KV_LORA = 256
B_QBLK = 128
B_IN = B_Q_LORA + B_KV_LORA + B_ROPE

D_FF_2 = 4 * D_MODEL

N_A = (DEPTH + 1) // 2
N_B = DEPTH // 2


def rms_norm(x, g):
    xf = x.astype(jnp.float32)
    y = xf * lax.rsqrt(jnp.mean(xf * xf, axis=-1, keepdims=True) + EPS)
    return (y * g.astype(jnp.float32)).astype(x.dtype)

def rope_angles(positions, rot_dim):
    inv = ROPE_THETA_2 ** (-jnp.arange(0, rot_dim, 2, dtype=jnp.float32) / rot_dim)
    ang = positions.astype(jnp.float32)[..., None] * inv
    return jnp.cos(ang), jnp.sin(ang)

def apply_rope_2(x, cos, sin):
    half = x.shape[-1] // 2
    x1 = x[..., :half].astype(jnp.float32)
    x2 = x[..., half:].astype(jnp.float32)
    c = cos[:, :, None, :]
    s = sin[:, :, None, :]
    return jnp.concatenate([x1 * c - x2 * s, x2 * c + x1 * s], axis=-1).astype(x.dtype)

def partial_rope(x, cos, sin, rot):
    return jnp.concatenate([apply_rope_2(x[..., :rot], cos, sin), x[..., rot:]], axis=-1)

def dsa_mixer(h, w_in, w_out, cos_a, sin_a, cos_i, sin_i):
    bsz, seq, _ = h.shape
    f32 = jnp.float32
    n_q = A_HEADS * A_HEAD_DIM
    n_kv = A_KV_HEADS * A_HEAD_DIM
    n_qi = IDX_HEADS * IDX_DIM
    cuts = [n_q, n_q + n_kv, n_q + 2 * n_kv, n_q + 2 * n_kv + n_qi, n_q + 2 * n_kv + n_qi + IDX_DIM]
    proj = h @ w_in
    q, k, v, qi, ki, wi = jnp.split(proj, cuts, axis=-1)
    q = partial_rope(q.reshape(bsz, seq, A_HEADS, A_HEAD_DIM), cos_a, sin_a, A_ROT)
    k = partial_rope(k.reshape(bsz, seq, A_KV_HEADS, A_HEAD_DIM), cos_a, sin_a, A_ROT)
    v = v.reshape(bsz, seq, A_KV_HEADS, A_HEAD_DIM)
    qi = partial_rope(qi.reshape(bsz, seq, IDX_HEADS, IDX_DIM), cos_i, sin_i, IDX_ROT)
    ki = partial_rope(ki[:, :, None, :], cos_i, sin_i, IDX_ROT)[:, :, 0, :]
    wi = wi.astype(f32) * IDX_WEIGHT_SCALE

    top_k = min(IDX_TOPK_MAX, seq // 4)
    group = A_HEADS // A_KV_HEADS
    scale = A_HEAD_DIM ** -0.5
    key_pos = jnp.arange(seq)

    def block(i):
        start = i * A_QBLK
        qb = lax.dynamic_slice_in_dim(q, start, A_QBLK, axis=1)
        qib = lax.dynamic_slice_in_dim(qi, start, A_QBLK, axis=1)
        wib = lax.dynamic_slice_in_dim(wi, start, A_QBLK, axis=1)
        q_pos = start + jnp.arange(A_QBLK)
        chunk_end = (q_pos // CHUNK + 1) * CHUNK
        logits = jnp.einsum('bthd,bsd->bths', qib, ki, preferred_element_type=f32)
        score = jnp.einsum('bths,bth->bts', jax.nn.relu(logits), wib)
        visible = key_pos[None, :] < chunk_end[:, None]
        score = jnp.where(visible[None], score, -jnp.inf)
        _, sel = lax.top_k(score, top_k)
        sel_ok = sel < chunk_end[None, :, None]
        flat = sel.reshape(bsz, A_QBLK * top_k)[:, :, None, None]
        kg = jnp.take_along_axis(k, flat, axis=1).reshape(bsz, A_QBLK, top_k, A_KV_HEADS, A_HEAD_DIM)
        vg = jnp.take_along_axis(v, flat, axis=1).reshape(bsz, A_QBLK, top_k, A_KV_HEADS, A_HEAD_DIM)
        qg = qb.reshape(bsz, A_QBLK, A_KV_HEADS, group, A_HEAD_DIM)
        s = jnp.einsum('btgrd,btkgd->btgrk', qg, kg, preferred_element_type=f32) * scale
        s = jnp.where(sel_ok[:, :, None, None, :], s, -jnp.inf)
        p = jax.nn.softmax(s, axis=-1)
        o = jnp.einsum('btgrk,btkgd->btgrd', p.astype(vg.dtype), vg, preferred_element_type=f32)
        return o.reshape(bsz, A_QBLK, A_HEADS * A_HEAD_DIM).astype(h.dtype)

    o = lax.map(block, jnp.arange(seq // A_QBLK))
    o = jnp.moveaxis(o, 0, 1).reshape(bsz, seq, A_HEADS * A_HEAD_DIM)
    return o @ w_out

def mla_mixer(h, w_in, q_norm, kv_norm, w_q_up, w_kv_up, w_out, cos_b, sin_b):
    bsz, seq, _ = h.shape
    f32 = jnp.float32
    proj = h @ w_in
    cq, ckv, kr = jnp.split(proj, [B_Q_LORA, B_Q_LORA + B_KV_LORA], axis=-1)
    cq = rms_norm(cq, q_norm)
    ckv = rms_norm(ckv, kv_norm)
    qf = (cq @ w_q_up).reshape(bsz, seq, B_HEADS, B_NOPE + B_ROPE)
    q_nope, q_rope = qf[..., :B_NOPE], apply_rope_2(qf[..., B_NOPE:], cos_b, sin_b)
    kr = apply_rope_2(kr[:, :, None, :], cos_b, sin_b)[:, :, 0, :]
    kv = (ckv @ w_kv_up).reshape(bsz, seq, B_HEADS, B_NOPE + B_V)
    k_nope, v = kv[..., :B_NOPE], kv[..., B_NOPE:]
    scale = (B_NOPE + B_ROPE) ** -0.5
    key_pos = jnp.arange(seq)

    def block(i):
        start = i * B_QBLK
        qn = lax.dynamic_slice_in_dim(q_nope, start, B_QBLK, axis=1)
        qr = lax.dynamic_slice_in_dim(q_rope, start, B_QBLK, axis=1)
        s = (jnp.einsum('bthd,bshd->bhts', qn, k_nope, preferred_element_type=f32)
             + jnp.einsum('bthd,bsd->bhts', qr, kr, preferred_element_type=f32)) * scale
        q_pos = start + jnp.arange(B_QBLK)
        chunk_end = (q_pos // CHUNK + 1) * CHUNK
        mask = key_pos[None, :] < chunk_end[:, None]
        s = jnp.where(mask[None, None], s, -jnp.inf)
        p = jax.nn.softmax(s, axis=-1)
        o = jnp.einsum('bhts,bshd->bthd', p.astype(v.dtype), v, preferred_element_type=f32)
        return o.reshape(bsz, B_QBLK, B_HEADS * B_V).astype(h.dtype)

    o = lax.map(block, jnp.arange(seq // B_QBLK))
    o = jnp.moveaxis(o, 0, 1).reshape(bsz, seq, B_HEADS * B_V)
    return o @ w_out

def squared_relu_mlp(h, w_up, w_down):
    a = jax.nn.relu(h @ w_up)
    return (a * a) @ w_down

def second_inputs(seed: int = 0) -> dict:
    key = jax.random.key(seed)
    ks = jax.random.split(key, 20)
    f32 = jnp.float32

    def nrm(k, shape, fan_in):
        return jax.random.normal(k, shape, f32) * (fan_in ** -0.5)

    def gain(k, shape):
        return 1.0 + 0.02 * jax.random.normal(k, shape, f32)

    x = jax.random.normal(ks[0], (BATCH, SEQ, D_MODEL), f32)
    starts = jax.random.randint(ks[1], (BATCH, 1), 0, 64, dtype=jnp.int32) * CHUNK
    positions = (starts + jnp.arange(SEQ, dtype=jnp.int32)[None, :]).astype(jnp.int32)
    return {
        'x': x,
        'positions': positions,
        'attn_norm': gain(ks[2], (DEPTH, D_MODEL)),
        'mlp_norm': gain(ks[3], (DEPTH, D_MODEL)),
        'a_w_in': nrm(ks[4], (N_A, D_MODEL, A_IN), D_MODEL),
        'a_w_out': nrm(ks[5], (N_A, A_HEADS * A_HEAD_DIM, D_MODEL), A_HEADS * A_HEAD_DIM),
        'b_w_in': nrm(ks[6], (N_B, D_MODEL, B_IN), D_MODEL),
        'b_q_norm': gain(ks[7], (N_B, B_Q_LORA)),
        'b_kv_norm': gain(ks[8], (N_B, B_KV_LORA)),
        'b_w_q_up': nrm(ks[9], (N_B, B_Q_LORA, B_HEADS * (B_NOPE + B_ROPE)), B_Q_LORA),
        'b_w_kv_up': nrm(ks[10], (N_B, B_KV_LORA, B_HEADS * (B_NOPE + B_V)), B_KV_LORA),
        'b_w_out': nrm(ks[11], (N_B, B_HEADS * B_V, D_MODEL), B_HEADS * B_V),
        'mlp_w_up': nrm(ks[12], (DEPTH, D_MODEL, D_FF_2), D_MODEL),
        'mlp_w_down': nrm(ks[13], (DEPTH, D_FF_2, D_MODEL), D_FF_2),
        'final_norm': gain(ks[14], (D_MODEL,)),
    }

def second_block(x, positions, attn_norm, mlp_norm, a_w_in, a_w_out, b_w_in, b_q_norm, b_kv_norm,
              b_w_q_up, b_w_kv_up, b_w_out, mlp_w_up, mlp_w_down, final_norm):
    cos_a, sin_a = rope_angles(positions, A_ROT)
    cos_i, sin_i = rope_angles(positions, IDX_ROT)
    cos_b, sin_b = rope_angles(positions, B_ROPE)
    for i in range(DEPTH):
        h = rms_norm(x, attn_norm[i])
        j = i // N_MIXERS
        if i % N_MIXERS == 0:
            x = x + dsa_mixer(h, a_w_in[j], a_w_out[j], cos_a, sin_a, cos_i, sin_i)
        else:
            x = x + mla_mixer(h, b_w_in[j], b_q_norm[j], b_kv_norm[j], b_w_q_up[j],
                              b_w_kv_up[j], b_w_out[j], cos_b, sin_b)
        h = rms_norm(x, mlp_norm[i])
        x = x + squared_relu_mlp(h, mlp_w_up[i], mlp_w_down[i])
    return rms_norm(x, final_norm)


def setup_inputs(seed=0):
    out = dict(first_inputs(seed))
    for name, value in second_inputs(seed + 1).items():
        if name != "x":
            out[name + "_2"] = value
    return out


def reference(
    x, meta_tokens, norm1_g, w_in, b_glu, conv_w, conv_b, conv_ln_g, conv_ln_b, lam_q1, lam_k1,
    lam_q2, lam_k2, subln_g, w_out, norm2_g, w_gate_up, w_down, final_g, positions_2,
    attn_norm_2, mlp_norm_2, a_w_in_2, a_w_out_2, b_w_in_2, b_q_norm_2, b_kv_norm_2, b_w_q_up_2,
    b_w_kv_up_2, b_w_out_2, mlp_w_up_2, mlp_w_down_2, final_norm_2,
):
    x = first_block(
        x, meta_tokens, norm1_g, w_in, b_glu, conv_w, conv_b, conv_ln_g, conv_ln_b, lam_q1,
        lam_k1, lam_q2, lam_k2, subln_g, w_out, norm2_g, w_gate_up, w_down, final_g,
    )
    return second_block(
        x, positions_2, attn_norm_2, mlp_norm_2, a_w_in_2, a_w_out_2, b_w_in_2, b_q_norm_2,
        b_kv_norm_2, b_w_q_up_2, b_w_kv_up_2, b_w_out_2, mlp_w_up_2, mlp_w_down_2, final_norm_2,
    )


_drawn_inputs = setup_inputs


def setup_inputs(seed=0):
    import zlib

    import numpy as np

    out = dict(_drawn_inputs(seed))
    spreads = {}
    factors = {'conv_ln_b': 2.708,
     'attn_norm_2': 2.738,
     'b_q_norm_2': 8.0,
     'b_kv_norm_2': 8.0,
     'final_norm_2': 2.862}
    for name, (base, spread) in spreads.items():
        noise = np.random.default_rng([zlib.crc32(name.encode()), seed]).standard_normal(out[name].shape)
        drawn = base * np.exp(spread * noise) if base else spread * noise
        out[name] = __import__('jax').numpy.asarray(drawn.astype(out[name].dtype))
    for name, factor in factors.items():
        out[name] = (out[name] * factor).astype(out[name].dtype)
    return out
```

```python
import math

import numpy as np

D = 1024
KC = D // 128
N_META = 16
SEQ = 512
TOK = N_META + SEQ
DEPTH = 2
HALF = TOK // 2
HEADS = 4
HD = 64
KW = 31
CC = 4
FF = 2816 // 128
FF_PARTS = [8, 8, FF - 16]
FF2_PARTS = 4
PAIRS = 8
IDX_HEADS = 8
TOPK = 128
SLOT = 8 * 128
RS = 4
RR = 2
EPS1, EPS2 = 1e-5, 1e-6
NEG = -1.0e30
TAKEN = -3.0e38
TWO_PI = 2.0 * math.pi
TWO_PI_PARTS = (6.28125, 0.0019350051879882812, TWO_PI - 6.28125 - 0.0019350051879882812)
PI_MAX = 3.1415925

def _param_columns():
    at, out = 0, {}
    for name, n in (("norm1", 16), ("norm2", 16), ("final", 8), ("attn2", 16), ("mlp2", 16), ("final2", 8),
                    ("bglu", 16), ("convw", DEPTH * CC * KW), ("convb", 8), ("lng", 8), ("lnb", 8), ("subg", 2),
                    ("qn", 3), ("kvn", 2), ("inva", 1), ("sgna", 1), ("invb", 1), ("sgnb", 1)):
        out[name] = at
        at += n
    return out, at


COL, NPARAM = _param_columns()


def plan():
    at = dict(S=0, T=0, O=0, F=0, G=0, Q=0, U=0, N=0, P=0, W=0, A=0)
    out = {}

    def phase(name, **used):
        out[name] = dict(at)
        for k, v in used.items():
            at[k] += v

    phase("load", O=8, Q=8, N=1)
    for l in range(DEPTH):
        units = HEADS * (5 if l == 0 else 4)
        phase(f"glu{l}", S=8, T=8, G=4)
        phase(f"qk{l}", S=8, T=8, O=8, G=8, F=8)
        phase(f"v{l}", S=4, O=5)
        phase(f"att{l}", U=units)
        phase(f"post{l}", O=8, P=9, F=4 + 4, G=4, W=8, A=6)
        phase(f"wo{l}", S=8, T=8, O=8, Q=8, N=1)
        for p, f in enumerate(FF_PARTS):
            phase(f"up{l}{p}", S=2 * f, T=2 * f, O=f, G=f, F=f)
            last = p == len(FF_PARTS) - 1
            more = dict(O=8, Q=8, N=1) if last and l == 0 else dict(Q=8, N=1) if last else {}
            phase(f"down{l}{p}", S=8, T=8, **more)
    phase("x2", F=8, O=8, Q=8, N=1)
    phase("qi", S=5, T=5, O=5, G=5, F=5)
    phase("q2", S=10, T=10, O=10, G=10, F=10)
    phase("v2", S=2, O=4)
    phase("att2", U=PAIRS * 4)
    phase("wo2", S=8, T=8, O=8, Q=8, N=1)
    for l in range(DEPTH):
        for p in range(FF2_PARTS):
            phase(f"mup{l}{p}", S=8, T=8, O=8, F=8)
            last = p == FF2_PARTS - 1
            more = dict(O=8, Q=8, N=1) if last and l == 0 else dict(Q=8, N=1) if last else {}
            phase(f"mdown{l}{p}", S=8, T=8, **more)
        if l == 0:
            phase("lat", S=7, T=7, O=7, F=1, W=5, P=1, A=1)
            for half in range(2):
                phase(f"lv{half}", S=2, O=4)
                phase(f"latt{half}", S=4, U=16, F=12, O=4 * 4)
            phase("wo3", S=8, T=8, O=8, Q=8, N=1)
    phase("end")
    return out


PL = plan()
DVE_TAPS = (CC - 1) * KW
NSLOT = PL["end"]["S"]


def build(nc, wstream, xT, params, lamv, tab1, masks, wiw, pos, out):
    import concourse.bass as bass
    from concourse import mybir
    from contextlib import ExitStack

    f32, f32r, i32 = mybir.dt.float32, mybir.dt.float32r, mybir.dt.int32
    ALU = mybir.AluOpType
    ACT = mybir.ActivationFunctionType
    AX = mybir.AxisListType
    MUL, ADD, SUB, MAX = ALU.mult, ALU.add, ALU.subtract, ALU.max
    V, SC, TE, GP = nc.vector, nc.scalar, nc.tensor, nc.gpsimd

    with ExitStack() as ctx:
        def sb(name, shape, dt=f32):
            return ctx.enter_context(nc.sbuf_tensor(name, shape, dt))

        def sem(name):
            return ctx.enter_context(nc.semaphore(name))

        RAW = sb("raw_weights", [128, RR, SLOT])
        WH = sb("weights_hi", [128, RS, SLOT], f32r)
        WL = sb("weights_lo", [128, RS, SLOT], f32r)
        XH = [sb(f"operand{i}_hi", [128, KC * TOK], f32r) for i in range(2)]
        XL = [sb(f"operand{i}_lo", [128, KC * TOK], f32r) for i in range(2)]
        VH = sb("values_hi", [128, 2560], f32r)
        VL = sb("values_lo", [128, 2560], f32r)
        AH = sb("probs_t_hi", [128, 2, 1024], f32r)
        AL = sb("probs_t_lo", [128, 2, 1024], f32r)
        H = sb("residual", [128, KC * TOK])
        PRB = sb("probs", [128, 2, 2, TOK])
        PRBF = PRB[:, :, :, :].rearrange("p a b n -> p (a b n)")
        Z = sb("conv_z", [128, CC, KW - 1 + TOK])
        ZF = Z[:, :, :].rearrange("p c n -> p (c n)")
        CACC = sb("conv_acc", [128, 2, TOK])
        ORAW = sb("head_out", [128, HEADS * TOK])
        TAB = sb("tables", [128, 4 * TOK])
        COS, SIN, COSR, SINR = 0, TOK, 2 * TOK, 3 * TOK
        R = sb("inv_rms", [128, TOK])
        RT = sb("inv_rms_by_token", [128, 8])
        TMP = sb("temps", [128, 4 * TOK])
        SQA = sb("square_sum", [128, TOK])
        CST = sb("consts", [128, 4 * 128])
        IDENT, ONES, MASK1, MASK2 = (CST[:, i * 128:(i + 1) * 128] for i in range(4))
        PAR = sb("params", [128, NPARAM])
        EPS = sb("eps", [128, 4])
        LAM = sb("lam", [128, 2 * DEPTH + 4])
        GS = sb("sub_gain", [128, DEPTH])
        NB = sb("neg_max", [128, 2, 2])
        MX = sb("row_max", [128, 2, 2])
        SS = sb("row_sum", [128, 2, 2])
        RL = sb("row_scale", [128, 2, 2])
        M8 = sb("top8", [128, 8])
        WIW = sb("idx_weights", [128, 64])
        WIH = sb("idx_weights_hi", [128, 64], f32r)
        WIL = sb("idx_weights_lo", [128, 64], f32r)
        POS = sb("positions", [128, SEQ], i32)
        WI = sb("idx_w_tok", [128, 4 * IDX_HEADS])
        PSUM = ctx.enter_context(nc.psum_tensor("psum", [128, 8, 512], f32))
        PF = PSUM[:, :, :].rearrange("p b n -> p (b n)")

        raw_loaded = [sem(f"raw_loaded{i}") for i in range(RR)]
        w_hi, w_lo, slot_done = sem("w_hi"), sem("w_lo"), sem("slot_done")
        tile_free = sem("tile_free")
        operand_hi, operand_lo = sem("operand_hi"), sem("operand_lo")
        f32_ready, act_result = sem("f32_ready"), sem("act_result")
        sq_ready, sq_added = sem("sq_ready"), sem("sq_added")
        norm_mm, std_ready, r_ready = sem("norm_mm"), sem("std_ready"), sem("r_ready")
        scores_ready, max_ready, probs_ready = sem("scores_ready"), sem("max_ready"), sem("probs_ready")
        mix_ready, tr_ready, th_ready, tl_ready = sem("mix_ready"), sem("tr_ready"), sem("th_ready"), sem("tl_ready")
        pv_ready, o_free = sem("pv_ready"), sem("o_free")
        stat_sq, stat_mm, stat_std = sem("stat_sq"), sem("stat_mm"), sem("stat_std")
        conv_done, tap_ready, tap_added, centered, idx_scores, idx_relu, idx_added = sem("conv_done"), sem("tap_ready"), sem("tap_added"), sem("centered"), sem("idx_scores"), sem("idx_relu"), sem("idx_added")
        wi_hi, wi_lo, wi_mm, wi_ready = sem("wi_hi"), sem("wi_lo"), sem("wi_mm"), sem("wi_ready")
        lam_dots, lam_exp, angles_ready, sines_ready = sem("lam_dots"), sem("lam_exp"), sem("angles_ready"), sem("sines_ready")
        lat_ready, oh_ready, map_done = sem("lat_ready"), sem("oh_ready"), sem("map_done")
        dve_chain, act_chain, pool_chain = sem("dve_chain"), sem("act_chain"), sem("pool_chain")
        h_loaded = [sem(f"h_loaded{i}") for i in range(KC)]
        par_loaded, tab_loaded, msk_loaded, lam_loaded, wiw_loaded, pos_loaded = (
            sem(n) for n in ("par_loaded", "tab_loaded", "msk_loaded", "lam_loaded", "wiw_loaded", "pos_loaded"))
        const_ready, out_ready, out_stored = sem("const_ready"), sem("out_ready"), sem("out_stored")

        def win(t2, off, full, rows=slice(0, 128)):
            if full:
                return t2[rows, bass.ds(off, TOK)].rearrange("p (b n) -> p b n", b=2)
            return t2[rows, bass.ds(off + N_META, SEQ)]

        def zwin(c, full):
            z = Z[:, c, KW - 1:]
            return z.rearrange("p (b n) -> p b n", b=2) if full else z[:, N_META:]

        def ps(bank, full, rows=slice(0, 128)):
            return PSUM[rows, bank:bank + 2, 0:HALF] if full else PSUM[rows, bank, 0:SEQ]

        def tile_bank(t, full):
            return 2 * (t % 2) if full else t % 4

        def depth(full):
            return 2 if full else 4

        def pieces(full):
            return [(0, HALF, 0), (HALF, HALF, 1)] if full else [(N_META, SEQ, 0)]

        def gain(name, i):
            return PAR[:, COL[name] + i:COL[name] + i + 1]

        def par(i):
            return (i % 2) * TOK

        def units1(l):
            out_ = []
            for hd in range(HEADS):
                if l == 0:
                    out_.append((hd, 0, N_META, N_META))
                for i in range(1, 5):
                    out_.append((hd, N_META + 128 * (i - 1), 128, N_META + 128 * i))
            return out_

        def score_at(u, c, nk):
            return 3 * 512 * (u % 2) + (0 if c == 0 else 1536 - nk)

        def acc_win(b, full):
            return CACC[:, b, :].rearrange("p (b n) -> p b n", b=2) if full else CACC[:, b, N_META:TOK]

        block = ctx.enter_context(nc.Block())

        @block.sync
        def _(sp):
            sp.dma_start(PAR[:, :], params).then_inc(par_loaded, 16)
            for c in range(KC):
                sp.dma_start(H[:, c * TOK:(c + 1) * TOK], xT[c * 128:(c + 1) * 128, :]).then_inc(h_loaded[c], 16)
                if c < RR:
                    sp.dma_start(RAW[:, c, :], wstream[c, :, :]).then_inc(raw_loaded[c], 16)
            sp.dma_start(TAB[:, 0:2 * TOK], tab1).then_inc(tab_loaded, 16)
            sp.dma_start(CST[:, 256:512], masks).then_inc(msk_loaded, 16)
            sp.dma_start(ORAW[:, 0:2 * 256], lamv[0:1, :].to_broadcast([128, 512])).then_inc(lam_loaded, 16)
            sp.dma_start(WIW[:, :], wiw).then_inc(wiw_loaded, 16)
            sp.dma_start(POS[:, :], pos[0:1, :].to_broadcast([128, SEQ])).then_inc(pos_loaded, 16)
            with sp.Fori(0, NSLOT // RR - 1) as i:
                for u in range(RR):
                    sp.wait_ge(w_lo, i * RR + (u + 1))
                    sp.dma_start(RAW[:, u, :], wstream[bass.ds(i * RR + (RR + u), 1), :, :].rearrange("a p n -> (a p) n")
                                 ).then_inc(raw_loaded[u], 16)
            for s in range(NSLOT // RR * RR, NSLOT):
                sp.wait_ge(w_lo, s - RR + 1)
                sp.dma_start(RAW[:, s % RR, :], wstream[s, :, :]).then_inc(raw_loaded[s % RR], 16)
            for c in range(KC):
                sp.wait_ge(out_ready, c + 1)
                sp.dma_start(out[c * 128:(c + 1) * 128, :], H[:, c * TOK + N_META:(c + 1) * TOK]).then_inc(out_stored, 16)
            sp.wait_ge(out_stored, 16 * KC)

        @block.gpsimd
        def _(pool):
            GP.memset(IDENT, 0.0).then_inc(pool_chain, 1)
            GP.memset(ONES, 1.0).then_inc(const_ready, 1)
            GP.memset(Z[:, :, 0:KW - 1], 0.0).then_inc(const_ready, 1)
            GP.memset(PRB[:, :, :, :], 0.0).then_inc(const_ready, 1)
            for i, e in enumerate((EPS1, EPS2, math.pi / 2)):
                GP.memset(EPS[:, i:i + 1], e).then_inc(const_ready, 1)
            pool.wait_ge(pool_chain, 1)
            GP.affine_select(out=IDENT, in_=IDENT, compare_op=ALU.not_equal, fill=1.0, base=0,
                             pattern=[[-1, 128]], channel_multiplier=1).then_inc(const_ready, 1)

            def weight_lo(s, d=0):
                if s >= NSLOT:
                    return
                pool.wait_ge(w_hi, s + 1 + d)
                GP.tensor_tensor(WL[:, s % RS, :], RAW[:, s % RR, :], WH[:, s % RS, :].bitcast(f32), SUB).then_inc(w_lo, 1)

            def square_sum(c, q, n, full):
                pool.wait_ge(sq_ready, q + 1)
                if c == 0:
                    if n > 0:
                        pool.wait_ge(norm_mm, n)
                    GP.tensor_copy(win(SQA, 0, full), win(TMP, par(c), full)).then_inc(sq_added, 1)
                else:
                    pool.wait_ge(sq_added, q)
                    GP.tensor_tensor(win(SQA, 0, full), win(SQA, 0, full), win(TMP, par(c), full), ADD).then_inc(sq_added, 1)

            def slots(name, n):
                for j in range(n):
                    weight_lo(PL[name]["S"] + j + RS)

            def slots_loop(name, n):
                b = PL[name]["S"]
                with pool.Fori(0, n // 4) as i:
                    for u in range(4):
                        weight_lo(b + u + RS, i * 4)

            def slots_norm(name, full):
                p = PL[name]
                for c in range(8):
                    weight_lo(p["S"] + c + RS)
                    square_sum(c, p["Q"] + c, p["N"], full)

            for s in range(2):
                weight_lo(s)
            for c in range(8):
                square_sum(c, c, 0, True)
                if c in (1, 3):
                    weight_lo(2 + c // 2)
            for l in range(DEPTH):
                full = l == 0
                slots(f"glu{l}", 8)
                slots(f"qk{l}", 8)
                slots(f"v{l}", 4)
                pool.wait_ge(operand_lo, PL[f"v{l}"]["O"])
                w, off = (TOK, 0) if full else (SEQ, N_META)
                for j in range(KW + 1):
                    if j < KW:
                        z, tap = Z[:, CC - 1, off + j:off + j + w], gain("convw", (l * CC + CC - 1) * KW + j)
                        if j == 0:
                            GP.tensor_scalar(TMP[:, 0:w], z, tap, gain("convb", 4 * l + CC - 1), MUL, ADD).then_inc(tap_added, 1)
                        else:
                            if j >= 3:
                                pool.wait_ge(tap_added, l * KW + j - 1)
                            GP.tensor_scalar(TMP[:, (1 + j % 2) * TOK:(1 + j % 2) * TOK + w], z, tap, None, MUL).then_inc(tap_ready, 1)
                    if j >= 2:
                        pool.wait_ge(tap_added, l * KW + j - 1)
                        pool.wait_ge(tap_ready, l * (KW - 1) + j - 1)
                        at = (1 + (j - 1) % 2) * TOK
                        GP.tensor_tensor(TMP[:, 0:w] if j < KW else Z[:, CC - 1, KW - 1 + off:KW - 1 + off + w],
                                         TMP[:, 0:w], TMP[:, at:at + w], ADD).then_inc(tap_added, 1)
                pool.wait_ge(stat_std, PL[f"post{l}"]["A"] + 5)
                for c in range(4):
                    GP.tensor_tensor(zwin(c, full), zwin(c, full), acc_win(0, full), SUB).then_inc(centered, 1)
                slots_norm(f"wo{l}", full)
                for p, f in enumerate(FF_PARTS):
                    slots_loop(f"up{l}{p}", 2 * f)
                    if p < len(FF_PARTS) - 1:
                        slots_loop(f"down{l}{p}", 8)
                    else:
                        slots_norm(f"down{l}{p}", full)
            for c in range(8):
                square_sum(c, PL["x2"]["Q"] + c, PL["x2"]["N"], False)
            slots("qi", 5)
            slots("q2", 10)
            slots("v2", 2)
            slots_norm("wo2", False)
            for l in range(DEPTH):
                for p in range(FF2_PARTS):
                    slots_loop(f"mup{l}{p}", 8)
                    if p < FF2_PARTS - 1:
                        slots_loop(f"mdown{l}{p}", 8)
                    else:
                        slots_norm(f"mdown{l}{p}", False)
                if l == 0:
                    slots("lat", 7)
                    for half in range(2):
                        slots(f"lv{half}", 2)
                        slots(f"latt{half}", 4)
                    slots_norm("wo3", False)

        @block.scalar
        def _(act):
            chain = [0]

            def link(ins):
                chain[0] += 1
                ins.then_inc(act_chain, 1)
                act.wait_ge(act_chain, chain[0])

            def weight_hi(s, d=0):
                if s >= NSLOT:
                    return
                act.wait_ge(raw_loaded[s % RR], 16 * (s // RR + 1) + d * (16 // RR))
                if s >= RS:
                    act.wait_ge(slot_done, s - RS + 1 + d)
                SC.activation(WH[:, s % RS, :], RAW[:, s % RR, :], ACT.Copy).then_inc(w_hi, 1)

            def prepare(c, q, src, gname, gi, dst, full, dyn=0):
                if q >= 2:
                    act.wait_ge(sq_added, q - 1)
                SC.activation(win(TMP, par(c), full), win(H, c * TOK, full), ACT.Square).then_inc(sq_ready, 1)
                if gname is not None:
                    SC.activation(win(XH[dst], c * TOK, full), win(H, c * TOK, full), ACT.Copy,
                                  scale=gain(gname, gi + c)).then_inc(operand_hi, 1)

            def norm(n, eps, full, by_token, width=D):
                act.wait_ge(norm_mm, n + 1)
                if by_token:
                    nt = 5 if full else 4
                    SC.activation(RT[:, 0:nt], PSUM[:, 7, 400:400 + nt], ACT.Sqrt, scale=1.0 / width, bias=EPS[:, eps:eps + 1]).then_inc(act_chain, 1)
                    chain[0] += 1
                SC.activation(win(R, 0, full), ps(6, full), ACT.Sqrt, scale=1.0 / width, bias=EPS[:, eps:eps + 1]).then_inc(std_ready, 1)

            def hi_of(o, f, dst, src):
                act.wait_ge(f32_ready, f + 1)
                SC.activation(dst, src, ACT.Copy).then_inc(operand_hi, 1)

            def rope_tile(j, p, bank, dst, doff, full, shift, window=True):
                act.wait_ge(slot_done, p["S"] + j + 1)
                moves = ((0, 32), (32, 0), (64, 96), (96, 64))
                for n, (to, fro) in enumerate(moves):
                    ins = SC.activation(win(TMP, 2 * TOK + par(j), full, slice(to, to + 32)), ps(bank, full, slice(fro, fro + 32)), ACT.Copy)
                    if n == 3:
                        ins.then_inc(act_result, 1)
                act.wait_ge(f32_ready, p["F"] + j + 1)
                src = win(TMP, par(j), full)
                d_ = win(dst, doff, full) if window else dst[:, doff:doff + SEQ]
                SC.activation(d_, src, ACT.Copy).then_inc(operand_hi, 1)

            def residual_phase(name, gname, gi, dst, full):
                p = PL[name]
                for c in range(8):
                    act.wait_ge(tile_free, p["T"] + c + 1)
                    prepare(c, p["Q"] + c, None, gname, gi, dst, full)
                    weight_hi(p["S"] + c + RS)

            def sines(n):
                act.wait_ge(angles_ready, n + 1)
                SC.activation(TAB[:, COS:COS + SEQ], TAB[:, COSR:COSR + SEQ], ACT.Sin).then_inc(sines_ready, 1)
                SC.activation(TAB[:, SIN:SIN + SEQ], TAB[:, SINR:SINR + SEQ], ACT.Sin).then_inc(sines_ready, 1)

            def down_loop(name):
                b = PL[name]["S"]
                with act.Fori(0, 2) as i:
                    for u in range(4):
                        weight_hi(b + u + RS, i * 4)

            act.wait_ge(const_ready, 7)
            for s in range(2):
                weight_hi(s)
            act.wait_ge(par_loaded, 16)
            for c in range(8):
                act.wait_ge(h_loaded[c], 16)
                prepare(c, c, None, "norm1", 0, 0, True)
                if c in (1, 3):
                    weight_hi(2 + c // 2)
            src = 0
            for l in range(DEPTH):
                full = l == 0
                dst = 1 - src
                norm(PL[f"glu{l}"]["N"] - 1, 0, True, True)
                p = PL[f"glu{l}"]
                for j in range(8):
                    if j % 2 == 0:
                        c = j // 2
                        act.wait_ge(tile_free, p["T"] + j + 1)
                        t = win(TMP, par(c), True)
                        SC.activation(t, t, ACT.Sigmoid, bias=gain("bglu", 8 * l + 4 + c)).then_inc(act_result, 1)
                    else:
                        act.wait_ge(slot_done, p["S"] + j + 1)
                    weight_hi(p["S"] + j + RS)
                p = PL[f"qk{l}"]
                for j in range(8):
                    rope_tile(j, p, tile_bank(p["T"] + j, True), XH[dst], j * TOK, True, 32)
                    weight_hi(p["S"] + j + RS)
                if l == 0:
                    act.wait_ge(lam_dots, 1)
                    SC.activation(LAM[:, 0:4], LAM[:, 0:4], ACT.Exp).then_inc(lam_exp, 1)
                p = PL[f"v{l}"]
                for s in range(4):
                    weight_hi(p["S"] + s + RS)
                act.wait_ge(slot_done, p["S"] + 4)
                for i in range(5):
                    rows = slice(0, N_META) if i == 0 else slice(0, 128)
                    SC.activation(VH[rows, i * 512:(i + 1) * 512], PSUM[rows, i, :], ACT.Copy, scale=RT[rows, i:i + 1]).then_inc(operand_hi, 1)
                units, u0 = units1(l), PL[f"att{l}"]["U"]
                for n in range(-1, len(units) + 1):
                    if 1 <= n <= len(units):
                        hd, q0, nq, nk = units[n - 1]
                        v = u0 + n - 1
                        act.wait_ge(tr_ready, v + 1)
                        if v >= 2:
                            act.wait_ge(pv_ready, v - 1)
                        ins = SC.activation(AH[0:N_META, v % 2, 512:512 + nq], PSUM[0:N_META, 7, 256:256 + nq], ACT.Copy)
                        if nq == 128:
                            ins = SC.activation(AH[:, v % 2, 0:nk - N_META], PSUM[:, 6, 0:nk - N_META], ACT.Copy)
                        ins.then_inc(th_ready, 1)
                    if n + 1 < len(units):
                        u = u0 + n + 1
                        hd, q0, nq, nk = units[n + 1]
                        act.wait_ge(max_ready, u + 1)
                        if u >= 2:
                            act.wait_ge(tr_ready, u - 1)
                        for c in range(2):
                            at = score_at(u, c, nk)
                            ins = SC.activation(PRB[0:nq, u % 2, c, 0:nk], PF[0:nq, at:at + nk], ACT.Exp,
                                                bias=NB[0:nq, u % 2, c:c + 1], accum_out=SS[0:nq, u % 2, c:c + 1])
                        ins.then_inc(probs_ready, 1)
                p = PL[f"post{l}"]
                act.wait_ge(o_free, u0 + len(units))
                act.wait_ge(tap_added, (l + 1) * KW)
                for e in range(4):
                    SC.activation(win(TMP, e * TOK, full), win(ORAW, e * TOK, full), ACT.Square).then_inc(stat_sq, 1)
                for e in range(4):
                    act.wait_ge(stat_mm, p["P"] + e + 1)
                    SC.activation(win(TMP, e * TOK, full), ps(2 * e, full), ACT.Sqrt, scale=1.0 / 128, bias=EPS[:, 0:1]).then_inc(stat_std, 1)
                act.wait_ge(stat_mm, p["P"] + 5)
                SC.activation(acc_win(0, full), ps(0, full), ACT.Copy, scale=1.0 / 512).then_inc(stat_std, 1)
                for e in range(4):
                    act.wait_ge(f32_ready, p["F"] + e + 1)
                    SC.activation(win(XH[src], e * TOK, full), win(ORAW, e * TOK, full), ACT.Copy, scale=GS[:, l:l + 1]).then_inc(operand_hi, 1)
                for c in range(4):
                    act.wait_ge(centered, 4 * l + c + 1)
                    SC.activation(win(PRBF, c * TOK, full), zwin(c, full), ACT.Square).then_inc(stat_sq, 1)
                act.wait_ge(stat_mm, p["P"] + 9)
                SC.activation(acc_win(1, full), ps(2, full), ACT.Sqrt, scale=1.0 / 512, bias=EPS[:, 0:1]).then_inc(stat_std, 1)
                for c in range(5):
                    if c < 4:
                        act.wait_ge(f32_ready, p["F"] + 4 + c + 1)
                        SC.activation(zwin(c, full), zwin(c, full), ACT.Silu, scale=gain("lng", 4 * l + c), bias=gain("lnb", 4 * l + c)).then_inc(act_result, 1)
                    if c >= 1:
                        act.wait_ge(act_result, p["G"] + c)
                        SC.activation(win(XH[src], (3 + c) * TOK, full), zwin(c - 1, full), ACT.Copy).then_inc(operand_hi, 1)
                residual_phase(f"wo{l}", "norm2", 8 * l, dst, full)
                norm(PL[f"wo{l}"]["N"], 0, full, False)
                for p_, f in enumerate(FF_PARTS):
                    p = PL[f"up{l}{p_}"]
                    with act.Fori(0, f // 2) as i:
                        for u in range(4):
                            c = u // 2
                            if u % 2 == 0:
                                act.wait_ge(tile_free, p["T"] + u + 1 + i * 4)
                                t = win(TMP, par(c), full)
                                SC.activation(t, t, ACT.Silu).then_inc(act_result, 1)
                            else:
                                hi_of(None, p["F"] + c + i * 2, win(XH[src], i * (2 * TOK) + c * TOK, full), win(TMP, 2 * TOK + par(c), full))
                            weight_hi(p["S"] + u + RS, i * 4)
                    if p_ < len(FF_PARTS) - 1:
                        down_loop(f"down{l}{p_}")
                    elif l == 0:
                        residual_phase(f"down{l}{p_}", "norm1", 8, dst, full)
                    else:
                        sines(0)
                        residual_phase(f"down{l}{p_}", None, 0, dst, full)
                src = dst
            p = PL["x2"]
            norm(p["N"] - 1, 0, False, False)
            for c in range(8):
                act.wait_ge(f32_ready, p["F"] + c + 1)
                prepare(c, p["Q"] + c, None, "attn2", 0, src, False)
            dst = 1 - src
            norm(PL["qi"]["N"] - 1, 1, False, True)
            act.wait_ge(wiw_loaded, 16)
            SC.activation(WIH[:, :], WIW[:, :], ACT.Copy).then_inc(wi_hi, 1)
            p = PL["qi"]
            for j in range(5):
                if j < 4:
                    rope_tile(j, p, tile_bank(p["T"] + j, False), XH[dst], j * TOK, False, 32)
                else:
                    rope_tile(j, p, tile_bank(p["T"] + j, False), VH, 2048, False, 32, window=False)
                weight_hi(p["S"] + j + RS)
            g0 = 0
            for i in range(1, 4):
                for hh in range(IDX_HEADS):
                    act.wait_ge(idx_scores, g0 + 1)
                    if g0 >= 2:
                        act.wait_ge(idx_added, g0 - 1)
                    SC.activation(PRB[:, g0 % 2, 0, 0:128 * (i + 1)], PSUM[:, 6 + g0 % 2, 0:128 * (i + 1)], ACT.Relu).then_inc(idx_relu, 1)
                    g0 += 1
            p = PL["q2"]
            for j in range(10):
                if j < 8:
                    rope_tile(j, p, tile_bank(p["T"] + j, False), XH[dst], j * TOK, False, 32)
                else:
                    rope_tile(j, p, tile_bank(p["T"] + j, False), VH, 1024 + (j - 8) * 512, False, 32, window=False)
                weight_hi(p["S"] + j + RS)
            p = PL["v2"]
            for s in range(2):
                weight_hi(p["S"] + s + RS)
            act.wait_ge(slot_done, p["S"] + 2)
            for i in range(4):
                SC.activation(VH[:, i * 256:(i + 1) * 256], PSUM[:, i, 0:256], ACT.Copy, scale=RT[:, i:i + 1]).then_inc(operand_hi, 1)

            def att2_exp(u, nk):
                act.wait_ge(max_ready, u + 1)
                act.wait_ge(tr_ready, u - 1)
                for c in range(2):
                    ins = SC.activation(PRB[:, u % 2, c, 0:nk], PSUM[:, 2 * (u % 2) + c, 0:nk], ACT.Exp,
                                        bias=NB[:, u % 2, c:c + 1], accum_out=SS[:, u % 2, c:c + 1])
                ins.then_inc(probs_ready, 1)

            def att2_th(v, nk):
                act.wait_ge(tr_ready, v + 1)
                act.wait_ge(pv_ready, v - 1)
                SC.activation(AH[:, v % 2, :].rearrange("p (c n) -> p c n", c=2)[:, :, 0:nk], PSUM[:, 4:6, 0:nk], ACT.Copy).then_inc(th_ready, 1)

            def att2_oh(w, xbuf, pair, qi):
                act.wait_ge(pv_ready, w + 1)
                o = pair * TOK + N_META + 128 * qi
                for c in range(2):
                    rows = slice(64 * c, 64 * c + 64)
                    at = 256 * (w % 2) + 128 * c
                    ins = SC.activation(XH[xbuf][rows, o:o + 128], PSUM[rows, 6, at:at + 128], ACT.Copy)
                ins.then_inc(oh_ready, 1)

            u0 = PL["att2"]["U"]
            for n in range(-1, PAIRS * 4 + 2):
                if 1 <= n <= PAIRS * 4:
                    att2_th(u0 + n - 1, 128 * ((n - 1) // PAIRS + 1))
                if n + 1 < PAIRS * 4:
                    att2_exp(u0 + n + 1, 128 * ((n + 1) // PAIRS + 1))
                if n >= 2:
                    att2_oh(u0 + n - 2, src, (n - 2) % PAIRS, (n - 2) // PAIRS)
            residual_phase("wo2", "mlp2", 0, dst, False)
            src, dst = dst, src
            for l in range(DEPTH):
                norm(PL[f"mup{l}0"]["N"] - 1, 1, False, False)
                for p_ in range(FF2_PARTS):
                    p = PL[f"mup{l}{p_}"]
                    with act.Fori(0, 2) as i:
                        for u in range(4):
                            hi_of(None, p["F"] + u + i * 4, win(XH[dst], i * (4 * TOK) + u * TOK, False), win(TMP, 2 * TOK + par(u), False))
                            weight_hi(p["S"] + u + RS, i * 4)
                    if p_ < FF2_PARTS - 1:
                        down_loop(f"mdown{l}{p_}")
                    elif l == 0:
                        sines(1)
                        residual_phase(f"mdown{l}{p_}", "attn2", 8, src, False)
                    else:
                        residual_phase(f"mdown{l}{p_}", None, 0, src, False)
                if l == 0:
                    norm(PL["lat"]["N"] - 1, 1, False, False)
                    p = PL["lat"]
                    for j in range(7):
                        if j < 5:
                            act.wait_ge(tile_free, p["T"] + j + 1)
                            SC.activation(ORAW[:, j * SEQ:(j + 1) * SEQ] if j < 4 else CACC[:, 0, 0:SEQ],
                                          TMP[:, par(j):par(j) + SEQ], ACT.Square).then_inc(stat_sq, 1)
                            g = gain("qn", j) if j < 3 else gain("kvn", j - 3)
                            SC.activation(win(XH[dst], j * TOK, False), TMP[:, par(j):par(j) + SEQ], ACT.Copy, scale=g).then_inc(operand_hi, 1)
                        elif j == 6:
                            act.wait_ge(f32_ready, p["F"] + 1)
                            SC.activation(win(XH[dst], 7 * TOK, False, slice(64, 128)), TMP[64:128, 2 * TOK:2 * TOK + SEQ], ACT.Copy).then_inc(operand_hi, 1)
                            SC.activation(VH[0:64, 2048:2560], TMP[0:64, 2 * TOK:2 * TOK + SEQ], ACT.Copy).then_inc(operand_hi, 1)
                        else:
                            act.wait_ge(slot_done, p["S"] + j + 1)
                        weight_hi(p["S"] + j + RS)
                    act.wait_ge(stat_mm, p["P"] + 1)
                    SC.activation(RT[:, 0:4], PSUM[:, 5, 0:4], ACT.Sqrt, scale=1.0 / 256, bias=EPS[:, 1:2]).then_inc(act_chain, 1)
                    SC.activation(R[:, 0:SEQ], PSUM[:, 7, 0:SEQ], ACT.Sqrt, scale=1.0 / 256, bias=EPS[:, 1:2]).then_inc(act_chain, 1)
                    SC.activation(TMP[:, 3 * TOK:3 * TOK + SEQ], PSUM[:, 6, 0:SEQ], ACT.Sqrt, scale=1.0 / 384, bias=EPS[:, 1:2]).then_inc(stat_std, 1)
                    for half in range(2):
                        p = PL[f"lv{half}"]
                        for s in range(2):
                            weight_hi(p["S"] + s + RS)
                        act.wait_ge(slot_done, p["S"] + 2)
                        act.wait_ge(lat_ready, 1)
                        for i in range(4):
                            SC.activation(VH[:, i * 512:(i + 1) * 512], PSUM[:, i, :], ACT.Copy, scale=RT[:, i:i + 1]).then_inc(operand_hi, 1)
                        p = PL[f"latt{half}"]
                        for n in range(16 + 2):
                            pr, qi = divmod(n, 4)
                            new = qi == 0 and n < 16
                            u = p["U"] + n
                            if new:
                                f = p["F"] + 3 * pr
                                hi_of(None, f, win(XH[dst], 5 * TOK, False), TMP[:, 0:SEQ])
                                hi_of(None, f + 1, win(XH[dst], 6 * TOK, False), TMP[:, TOK:TOK + SEQ])
                                hi_of(None, f + 2, win(XH[dst], 7 * TOK, False, slice(0, 64)), TMP[0:64, 2 * TOK:2 * TOK + SEQ])
                                SC.activation(VH[64:128, 2048:2560], TMP[64:128, 2 * TOK:2 * TOK + SEQ], ACT.Copy).then_inc(operand_hi, 1)
                                weight_hi(p["S"] + pr + RS)
                                if n >= 1:
                                    att2_th(u - 1, 512)
                                if n >= 2:
                                    att2_oh(u - 2, src, 4 * half + (n - 2) // 4, (n - 2) % 4)
                                att2_exp(u, 128)
                                att2_exp(u + 1, 256)
                            else:
                                if n <= 16:
                                    att2_th(u - 1, 128 * ((n - 1) % 4 + 1))
                                if n < 16 and qi < 3:
                                    att2_exp(u + 1, 128 * (qi + 2))
                                if n >= 2:
                                    att2_oh(u - 2, src, 4 * half + (n - 2) // 4, (n - 2) % 4)
                    residual_phase("wo3", "mlp2", 8, dst, False)
                    src, dst = dst, src
            norm(PL["end"]["N"] - 1, 1, False, False)

        @block.vector
        def _(dve):
            chain = [0]

            def link(ins):
                chain[0] += 1
                ins.then_inc(dve_chain, 1)
                dve.wait_ge(dve_chain, chain[0])

            def r32(ap):
                return ap.bitcast(f32)

            def lo_gain(o, dst, full, c, gname, gi):
                dve.wait_ge(operand_hi, o + 1)
                V.scalar_tensor_tensor(win(XL[dst], c * TOK, full), win(H, c * TOK, full), gain(gname, gi + c),
                                       r32(win(XH[dst], c * TOK, full)), MUL, SUB).then_inc(operand_lo, 1)

            def lo_of(o, dst, src, hi):
                dve.wait_ge(operand_hi, o + 1)
                V.tensor_tensor(dst, src, r32(hi), SUB).then_inc(operand_lo, 1)

            def norm(n, full, by_token):
                dve.wait_ge(std_ready, n + 1)
                if by_token:
                    nt = 5 if full else 4
                    V.reciprocal(RT[:, 0:nt], RT[:, 0:nt]).then_inc(dve_chain, 1)
                    chain[0] += 1
                V.reciprocal(win(R, 0, full), win(R, 0, full)).then_inc(r_ready, 1)
                dve.wait_ge(r_ready, n + 1)

            def scale_tables(full):
                for a, b in ((COS, COSR), (SIN, SINR)):
                    if full:
                        s_, d_, r_ = TAB[:, a:a + TOK], TAB[:, b:b + TOK], R[:, :]
                    else:
                        s_, d_, r_ = TAB[:, a:a + SEQ], TAB[:, b:b + SEQ], R[:, N_META:TOK]
                    link(V.tensor_tensor(d_, s_, r_, MUL))

            def sci(i):
                at = (0, 0, 256, 640)[i]
                return ZF[:, at:at + 128 * (i + 1)]

            def oh_count(w):
                return w - PL["att2"]["U"]

            def angles(inv, sgn):
                ang, k_, r_ = (TMP[:, m * TOK:m * TOK + SEQ] for m in range(3))
                ki = ORAW[:, 0:SEQ].bitcast(i32)
                dve.wait_ge(pos_loaded, 16)
                link(V.tensor_copy(ang, POS[:, :]))
                link(V.tensor_scalar(ang, ang, gain(inv, 0), None, MUL))
                link(V.tensor_scalar(ki, ang, 1.0 / TWO_PI, None, MUL))
                link(V.tensor_copy(k_, ki))
                for part in TWO_PI_PARTS:
                    link(V.scalar_tensor_tensor(ang, k_, -part, ang, MUL, ADD))
                link(V.tensor_scalar(r_, ang, math.pi / 2, -TWO_PI, ALU.is_gt, MUL))
                link(V.scalar_tensor_tensor(r_, ang, math.pi / 2, r_, ADD, ADD))
                link(V.tensor_scalar(TAB[:, COSR:COSR + SEQ], r_, PI_MAX, -PI_MAX, ALU.min, MAX))
                link(V.tensor_scalar(ang, ang, gain(sgn, 0), None, MUL))
                V.tensor_scalar(TAB[:, SINR:SINR + SEQ], ang, PI_MAX, -PI_MAX, ALU.min, MAX).then_inc(angles_ready, 1)

            def rope_tile(j, p, bank, scale, dst_lo, dst_hi, full):
                if full:
                    cosr, sinr = (TAB[:, b:b + TOK].rearrange("p (b n) -> p b n", b=2) for b in (COSR, SINR))
                else:
                    cosr, sinr = (TAB[:, b:b + SEQ] for b in (COSR, SINR))
                t, rr = win(TMP, par(j), full), win(TMP, 2 * TOK + par(j), full)
                dve.wait_ge(act_result, p["G"] + j + 1)
                V.scalar_tensor_tensor(rr, rr, scale, sinr, MUL, MUL).then_inc(dve_chain, 1)
                chain[0] += 1
                V.scalar_tensor_tensor(t, ps(bank, full), scale, cosr, MUL, MUL).then_inc(tile_free, 1)
                dve.wait_ge(dve_chain, chain[0])
                dve.wait_ge(tile_free, p["T"] + j + 1)
                V.tensor_tensor(t, t, rr, ADD).then_inc(f32_ready, 1)
                lo_of(p["O"] + j, dst_lo, t, dst_hi)

            def conv_taps(l, n0, n1, full):
                w, off = (TOK, 0) if full else (SEQ, N_META)
                for n in range(n0, min(n1, DVE_TAPS)):
                    paired = n < 2 * KW
                    j, c = divmod(n, 2) if paired else (n - 2 * KW, 2)
                    if n >= 2:
                        dve.wait_ge(conv_done, l * DVE_TAPS + n - paired)
                    z, acc = Z[:, c, off + j:off + j + w], CACC[:, c % 2, 0:w]
                    tap = gain("convw", (l * CC + c) * KW + j)
                    if j == 0:
                        V.tensor_scalar(acc, z, tap, gain("convb", 4 * l + c), MUL, ADD).then_inc(conv_done, 1)
                    else:
                        V.scalar_tensor_tensor(acc if j < KW - 1 else z, z, tap, acc, MUL, ADD).then_inc(conv_done, 1)

            def residual_phase(name, gname, gi, dst, full):
                p = PL[name]
                for c in range(8):
                    dve.wait_ge(slot_done, p["S"] + c + 1)
                    h = win(H, c * TOK, full)
                    V.tensor_tensor(h, h, ps(tile_bank(p["T"] + c, full), full), ADD).then_inc(tile_free, 1)
                    if gname is not None:
                        if c == 0:
                            dve.wait_ge(tile_free, p["T"] + 1)
                        lo_gain(p["O"] + c, dst, full, c, gname, gi)

            def down_loop(name, full):
                p = PL[name]
                with dve.Fori(0, 2) as i:
                    for u in range(4):
                        dve.wait_ge(slot_done, p["S"] + u + 1 + i * 4)
                        h = win(H, i * (4 * TOK) + u * TOK, full)
                        V.tensor_tensor(h, h, ps(tile_bank(p["T"] + u, full), full), ADD).then_inc(tile_free, 1)

            dve.wait_ge(const_ready, 7)
            dve.wait_ge(par_loaded, 16)
            for c in range(8):
                dve.wait_ge(h_loaded[c], 16)
                lo_gain(c, 0, True, c, "norm1", 0)
            src = 0
            for l in range(DEPTH):
                full = l == 0
                dst = 1 - src
                norm(PL[f"glu{l}"]["N"] - 1, True, True)
                p = PL[f"glu{l}"]
                for j in range(8):
                    c = j // 2
                    dve.wait_ge(slot_done, p["S"] + j + 1)
                    t = win(TMP, (j % 2) * 2 * TOK + par(c), True)
                    V.tensor_tensor(t, ps(tile_bank(p["T"] + j, True), True), win(R, 0, True), MUL).then_inc(tile_free, 1)
                    if j % 2:
                        dve.wait_ge(tile_free, p["T"] + j + 1)
                        dve.wait_ge(act_result, p["G"] + c + 1)
                        link(V.scalar_tensor_tensor(zwin(c, True), t, gain("bglu", 8 * l + c), win(TMP, par(c), True), ADD, MUL))
                if l == 0:
                    dve.wait_ge(tab_loaded, 16)
                scale_tables(True)
                if l == 0:
                    dve.wait_ge(lam_loaded, 16)
                    dve.wait_ge(msk_loaded, 16)
                    for m in range(2 * DEPTH):
                        q_ = ORAW[:, m * 128:m * 128 + 64]
                        link(V.tensor_tensor(q_, q_, ORAW[:, m * 128 + 64:m * 128 + 128], MUL))
                        ins = V.reduce_sum(LAM[:, m:m + 1], q_, axis=AX.X)
                    ins.then_inc(lam_dots, 1)
                p = PL[f"qk{l}"]
                taps = 0
                for j in range(8):
                    rope_tile(j, p, tile_bank(p["T"] + j, True), HD ** -0.5 if j < 4 else 1.0,
                              win(XL[dst], j * TOK, True), win(XH[dst], j * TOK, True), True)
                    conv_taps(l, taps, taps + 5, full)
                    taps += 5
                p = PL[f"v{l}"]
                for i in range(5):
                    rows = slice(0, N_META) if i == 0 else slice(0, 128)
                    at = slice(i * 512, (i + 1) * 512)
                    dve.wait_ge(operand_hi, p["O"] + i + 1)
                    V.scalar_tensor_tensor(VL[rows, at], PSUM[rows, i, :], RT[rows, i:i + 1], r32(VH[rows, at]), MUL, SUB).then_inc(operand_lo, 1)
                if l == 0:
                    dve.wait_ge(lam_exp, 1)
                    for m in range(DEPTH):
                        init = 0.8 - 0.6 * math.exp(-0.3 * m)
                        link(V.tensor_tensor(LAM[:, 4 + m:5 + m], LAM[:, 2 * m + 1:2 * m + 2], LAM[:, 2 * m:2 * m + 1], SUB))
                        link(V.tensor_scalar(LAM[:, 4 + m:5 + m], LAM[:, 4 + m:5 + m], init, None, SUB))
                        link(V.tensor_scalar(GS[:, m:m + 1], gain("subg", m), 1.0 - init, None, MUL))
                units, u0 = units1(l), PL[f"att{l}"]["U"]
                per = -(-(DVE_TAPS - taps) // (len(units) + 2))
                for n in range(-1, len(units) + 2):
                    if n + 1 < len(units):
                        u = u0 + n + 1
                        hd, q0, nq, nk = units[n + 1]
                        dve.wait_ge(scores_ready, u + 1)
                        for c in range(2):
                            e = score_at(u, c, nk) + nk
                            V.tensor_tensor(PF[0:nq, e - nq:e], PF[0:nq, e - nq:e], MASK1[0:nq, 0:nq], ADD).then_inc(dve_chain, 1)
                            chain[0] += 1
                        dve.wait_ge(dve_chain, chain[0])
                        for c in range(2):
                            at = score_at(u, c, nk)
                            ins = V.tensor_reduce(NB[0:nq, u % 2, c:c + 1], PF[0:nq, at:at + nk], axis=AX.X, op=MAX, negate=True)
                        ins.then_inc(max_ready, 1)
                    if n >= 2:
                        hd, q0, nq, nk = units[n - 2]
                        w = u0 + n - 2
                        dve.wait_ge(pv_ready, w + 1)
                        V.tensor_copy(ORAW[:, hd * TOK + q0:hd * TOK + q0 + nq], PSUM[:, 7, 128 * (w % 2):128 * (w % 2) + nq]).then_inc(o_free, 1)
                    if 0 <= n < len(units):
                        u = u0 + n
                        hd, q0, nq, nk = units[n]
                        dve.wait_ge(probs_ready, u + 1)
                        link(V.reciprocal(RL[0:nq, u % 2, :], SS[0:nq, u % 2, :]))
                        link(V.tensor_tensor(RL[0:nq, u % 2, 1:2], RL[0:nq, u % 2, 1:2], LAM[0:nq, 4 + l:5 + l], MUL))
                        link(V.tensor_scalar(PRB[0:nq, u % 2, 1, 0:nk], PRB[0:nq, u % 2, 1, 0:nk], RL[0:nq, u % 2, 1:2], None, MUL))
                        V.scalar_tensor_tensor(PRB[0:nq, u % 2, 0, 0:nk], PRB[0:nq, u % 2, 0, 0:nk], RL[0:nq, u % 2, 0:1],
                                               PRB[0:nq, u % 2, 1, 0:nk], MUL, ADD).then_inc(mix_ready, 1)
                    if 1 <= n <= len(units):
                        hd, q0, nq, nk = units[n - 1]
                        v = u0 + n - 1
                        dve.wait_ge(th_ready, v + 1)
                        ins = V.tensor_tensor(AL[0:N_META, v % 2, 512:512 + nq], PSUM[0:N_META, 7, 256:256 + nq],
                                              r32(AH[0:N_META, v % 2, 512:512 + nq]), SUB)
                        if nq == 128:
                            ins = V.tensor_tensor(AL[:, v % 2, 0:nk - N_META], PSUM[:, 6, 0:nk - N_META],
                                                  r32(AH[:, v % 2, 0:nk - N_META]), SUB)
                        ins.then_inc(tl_ready, 1)
                    conv_taps(l, taps, taps + per, full)
                    taps = min(taps + per, DVE_TAPS)
                assert taps == DVE_TAPS
                p = PL[f"post{l}"]
                for e in range(4):
                    dve.wait_ge(stat_std, p["A"] + e + 1)
                    rr, o_ = win(TMP, e * TOK, full), win(ORAW, e * TOK, full)
                    link(V.reciprocal(rr, rr))
                    V.tensor_tensor(o_, o_, rr, MUL).then_inc(f32_ready, 1)
                for e in range(4):
                    dve.wait_ge(operand_hi, p["O"] + e + 1)
                    V.scalar_tensor_tensor(win(XL[src], e * TOK, full), win(ORAW, e * TOK, full), GS[:, l:l + 1],
                                           r32(win(XH[src], e * TOK, full)), MUL, SUB).then_inc(operand_lo, 1)
                dve.wait_ge(stat_std, p["A"] + 6)
                dve.wait_ge(centered, 4 * (l + 1))
                rr = acc_win(1, full)
                link(V.reciprocal(rr, rr))
                for c in range(4):
                    V.tensor_tensor(zwin(c, full), zwin(c, full), rr, MUL).then_inc(f32_ready, 1)
                for c in range(4):
                    lo_of(p["O"] + 4 + c, win(XL[src], (4 + c) * TOK, full), zwin(c, full), win(XH[src], (4 + c) * TOK, full))
                residual_phase(f"wo{l}", "norm2", 8 * l, dst, full)
                norm(PL[f"wo{l}"]["N"], full, False)
                for p_, f in enumerate(FF_PARTS):
                    p = PL[f"up{l}{p_}"]
                    with dve.Fori(0, f // 2) as i:
                        for u in range(4):
                            c = u // 2
                            dve.wait_ge(slot_done, p["S"] + u + 1 + i * 4)
                            t = win(TMP, (u % 2) * 2 * TOK + par(c), full)
                            V.tensor_tensor(t, ps(tile_bank(p["T"] + u, full), full), win(R, 0, full), MUL).then_inc(tile_free, 1)
                            if u % 2:
                                dve.wait_ge(tile_free, p["T"] + u + 1 + i * 4)
                                dve.wait_ge(act_result, p["G"] + c + 1 + i * 2)
                                V.tensor_tensor(t, t, win(TMP, par(c), full), MUL).then_inc(f32_ready, 1)
                                lo_of(p["O"] + c + i * 2, win(XL[src], i * (2 * TOK) + c * TOK, full), t, win(XH[src], i * (2 * TOK) + c * TOK, full))
                    if p_ < len(FF_PARTS) - 1:
                        down_loop(f"down{l}{p_}", full)
                    elif l == 0:
                        residual_phase(f"down{l}{p_}", "norm1", 8, dst, full)
                    else:
                        angles("inva", "sgna")
                        residual_phase(f"down{l}{p_}", None, 0, dst, full)
                src = dst
            p = PL["x2"]
            norm(p["N"] - 1, False, False)
            for c in range(9):
                if c < 8:
                    h = win(H, c * TOK, False)
                    V.scalar_tensor_tensor(h, h, gain("final", c), win(R, 0, False), MUL, MUL).then_inc(f32_ready, 1)
                if c >= 1:
                    dve.wait_ge(f32_ready, p["F"] + c)
                    lo_gain(p["O"] + c - 1, src, False, c - 1, "attn2", 0)
            dst = 1 - src
            dve.wait_ge(wi_hi, 1)
            V.tensor_tensor(WIL[:, :], WIW[:, :], r32(WIH[:, :]), SUB).then_inc(wi_lo, 1)
            norm(PL["qi"]["N"] - 1, False, True)
            dve.wait_ge(sines_ready, 2)
            scale_tables(False)
            p = PL["qi"]
            for j in range(5):
                lo_, hi_ = ((win(b, j * TOK, False) for b in (XL[dst], XH[dst])) if j < 4 else (b[:, 2048:2560] for b in (VL, VH)))
                rope_tile(j, p, tile_bank(p["T"] + j, False), 1.0, lo_, hi_, False)
            dve.wait_ge(wi_mm, 1)
            for i in range(4):
                ins = V.tensor_scalar(WI[:, i * 8:(i + 1) * 8], PSUM[:, 5, i * 8:(i + 1) * 8], RT[:, i:i + 1],
                                      (IDX_HEADS ** -0.5) * (HD ** -0.5), MUL, MUL)
            link(ins)
            g0 = 0
            for i in range(1, 4):
                nk = 128 * (i + 1)
                sc = sci(i)
                for hh in range(IDX_HEADS):
                    dve.wait_ge(idx_relu, g0 + 1)
                    w = WI[:, i * 8 + hh:i * 8 + hh + 1]
                    if hh == 0:
                        V.tensor_scalar(sc, PRB[:, g0 % 2, 0, 0:nk], w, None, MUL).then_inc(idx_added, 1)
                    else:
                        dve.wait_ge(idx_added, g0)
                        V.scalar_tensor_tensor(sc, PRB[:, g0 % 2, 0, 0:nk], w, sc, MUL, ADD).then_inc(idx_added, 1)
                    g0 += 1
            dve.wait_ge(idx_added, g0)
            for i in range(1, 4):
                sc = sci(i)[:, 128 * i:128 * (i + 1)]
                link(V.tensor_tensor(sc, sc, MASK2, ADD))
            rounds = TOPK // 8
            PER_TILE, PER_UNIT = 3, 1

            def topk_rounds(n0, n1):
                for n in range(n0, min(n1, 3 * rounds)):
                    sc = sci(1 + n // rounds)
                    link(V.max(M8[:, :], sc))
                    link(V.match_replace(sc, M8[:, :], sc, TAKEN))

            p = PL["q2"]
            for j in range(10):
                if j < 8:
                    lo_, hi_ = (win(b, j * TOK, False) for b in (XL[dst], XH[dst]))
                else:
                    lo_, hi_ = (b[:, 1024 + (j - 8) * 512:1536 + (j - 8) * 512] for b in (VL, VH))
                rope_tile(j, p, tile_bank(p["T"] + j, False), HD ** -0.5 if j < 8 else 1.0, lo_, hi_, False)
                topk_rounds(PER_TILE * j, PER_TILE * (j + 1))

            def mask_of(i):
                link(V.tensor_scalar(sci(i), sci(i), 0.5 * TAKEN, NEG, ALU.is_ge, MUL))

            p = PL["v2"]
            for i in range(4):
                at = slice(i * 256, (i + 1) * 256)
                dve.wait_ge(operand_hi, p["O"] + i + 1)
                V.scalar_tensor_tensor(VL[:, at], PSUM[:, i, 0:256], RT[:, i:i + 1], r32(VH[:, at]), MUL, SUB).then_inc(operand_lo, 1)

            def att2_max(u, qi, selected):
                nk, b = 128 * (qi + 1), 2 * (u % 2)
                dve.wait_ge(scores_ready, u + 1)
                if selected and qi > 0:
                    for c in range(2):
                        V.tensor_tensor(PSUM[:, b + c, 0:nk], PSUM[:, b + c, 0:nk], sci(qi), ADD).then_inc(dve_chain, 1)
                else:
                    for c in range(2):
                        V.tensor_tensor(PSUM[:, b + c, nk - 128:nk], PSUM[:, b + c, nk - 128:nk], MASK2, ADD).then_inc(dve_chain, 1)
                chain[0] += 2
                dve.wait_ge(dve_chain, chain[0])
                V.tensor_reduce(NB[:, u % 2, :], PSUM[:, b:b + 2, 0:nk], axis=AX.X, op=MAX, negate=True).then_inc(max_ready, 1)

            def att2_tl(v, nk):
                dve.wait_ge(th_ready, v + 1)
                hi, lo = (b[:, v % 2, :].rearrange("p (c n) -> p c n", c=2)[:, :, 0:nk] for b in (AH, AL))
                V.tensor_tensor(lo, PSUM[:, 4:6, 0:nk], r32(hi), SUB).then_inc(tl_ready, 1)

            def att2_mix(u, nk):
                dve.wait_ge(probs_ready, u + 1)
                link(V.reciprocal(RL[:, u % 2, :], SS[:, u % 2, :]))
                for c in range(2):
                    ins = V.tensor_scalar(PRB[:, u % 2, c, 0:nk], PRB[:, u % 2, c, 0:nk], RL[:, u % 2, c:c + 1], None, MUL)
                ins.then_inc(mix_ready, 1)

            def att2_ol(w, xbuf, pair, qi):
                dve.wait_ge(oh_ready, oh_count(w) + 1)
                o = pair * TOK + N_META + 128 * qi
                for c in range(2):
                    rows = slice(64 * c, 64 * c + 64)
                    at = 256 * (w % 2) + 128 * c
                    ins = V.tensor_tensor(XL[xbuf][rows, o:o + 128], PSUM[rows, 6, at:at + 128], r32(XH[xbuf][rows, o:o + 128]), SUB)
                ins.then_inc(o_free, 1)

            u0 = PL["att2"]["U"]
            for n in range(-1, PAIRS * 4 + 2):
                if n + 1 < PAIRS * 4:
                    if n + 1 in (PAIRS, 2 * PAIRS, 3 * PAIRS):
                        mask_of((n + 1) // PAIRS)
                    att2_max(u0 + n + 1, (n + 1) // PAIRS, True)
                if 0 <= n < PAIRS * 4:
                    att2_mix(u0 + n, 128 * (n // PAIRS + 1))
                if 1 <= n <= PAIRS * 4:
                    att2_tl(u0 + n - 1, 128 * ((n - 1) // PAIRS + 1))
                if n >= 0:
                    topk_rounds(10 * PER_TILE + PER_UNIT * n, 10 * PER_TILE + PER_UNIT * (n + 1))
                if n >= 2:
                    att2_ol(u0 + n - 2, src, (n - 2) % PAIRS, (n - 2) // PAIRS)
            residual_phase("wo2", "mlp2", 0, dst, False)
            src, dst = dst, src
            for l in range(DEPTH):
                norm(PL[f"mup{l}0"]["N"] - 1, False, False)
                for p_ in range(FF2_PARTS):
                    p = PL[f"mup{l}{p_}"]
                    with dve.Fori(0, 2) as i:
                        for u in range(4):
                            dve.wait_ge(slot_done, p["S"] + u + 1 + i * 4)
                            t, m = win(TMP, par(u), False), win(TMP, 2 * TOK + par(u), False)
                            V.tensor_tensor(t, ps(tile_bank(p["T"] + u, False), False), win(R, 0, False), MUL).then_inc(tile_free, 1)
                            dve.wait_ge(tile_free, p["T"] + u + 1 + i * 4)
                            V.scalar_tensor_tensor(m, t, 0.0, t, MAX, MUL).then_inc(f32_ready, 1)
                            at = i * (4 * TOK) + u * TOK
                            lo_of(p["O"] + u + i * 4, win(XL[dst], at, False), m, win(XH[dst], at, False))
                    if p_ < FF2_PARTS - 1:
                        down_loop(f"mdown{l}{p_}", False)
                    elif l == 0:
                        angles("invb", "sgnb")
                        residual_phase(f"mdown{l}{p_}", "attn2", 8, src, False)
                    else:
                        residual_phase(f"mdown{l}{p_}", None, 0, src, False)
                if l == 0:
                    norm(PL["lat"]["N"] - 1, False, False)
                    dve.wait_ge(sines_ready, 4)
                    scale_tables(False)
                    p = PL["lat"]
                    for j in range(7):
                        dve.wait_ge(slot_done, p["S"] + j + 1)
                        src_ps = ps(tile_bank(p["T"] + j, False), False)
                        if j < 5:
                            t = TMP[:, par(j):par(j) + SEQ]
                            V.tensor_tensor(t, src_ps, win(R, 0, False), MUL).then_inc(tile_free, 1)
                            g = gain("qn", j) if j < 3 else gain("kvn", j - 3)
                            dve.wait_ge(tile_free, p["T"] + j + 1)
                            dve.wait_ge(operand_hi, p["O"] + j + 1)
                            V.scalar_tensor_tensor(win(XL[dst], j * TOK, False), t, g, r32(win(XH[dst], j * TOK, False)), MUL, SUB).then_inc(operand_lo, 1)
                        else:
                            tab = TAB[:, COSR:COSR + SEQ] if j == 5 else TAB[:, SINR:SINR + SEQ]
                            V.tensor_tensor(TMP[:, (j - 3) * TOK:(j - 3) * TOK + SEQ], src_ps, tab, MUL).then_inc(tile_free, 1)
                    dve.wait_ge(tile_free, p["T"] + 7)
                    kr = TMP[:, 2 * TOK:2 * TOK + SEQ]
                    V.tensor_tensor(kr, kr, TMP[:, 3 * TOK:3 * TOK + SEQ], ADD).then_inc(f32_ready, 1)
                    dve.wait_ge(f32_ready, p["F"] + 1)
                    lo_of(p["O"] + 5, win(XL[dst], 7 * TOK, False, slice(64, 128)), kr[64:128, :], win(XH[dst], 7 * TOK, False, slice(64, 128)))
                    lo_of(p["O"] + 6, VL[0:64, 2048:2560], kr[0:64, :], VH[0:64, 2048:2560])
                    dve.wait_ge(stat_std, p["A"] + 1)
                    link(V.reciprocal(RT[:, 0:4], RT[:, 0:4]))
                    link(V.reciprocal(R[:, 0:SEQ], R[:, 0:SEQ]))
                    rq = TMP[:, 3 * TOK:3 * TOK + SEQ]
                    link(V.reciprocal(rq, rq))
                    sc96 = 96 ** -0.5
                    for rows, tab_, to in ((slice(64, 96), COS, COSR), (slice(96, 128), SIN, COSR), (slice(0, 32), COS, SINR), (slice(32, 64), SIN, SINR)):
                        V.scalar_tensor_tensor(TAB[rows, to:to + SEQ], TAB[rows, tab_:tab_ + SEQ], sc96, rq[rows, :], MUL, MUL)
                    V.tensor_scalar(TAB[0:64, COSR:COSR + SEQ], rq[0:64, :], sc96, None, MUL)
                    V.tensor_scalar(TAB[64:128, SINR:SINR + SEQ], rq[64:128, :], sc96, None, MUL).then_inc(lat_ready, 1)
                    dve.wait_ge(lat_ready, 1)
                    for half in range(2):
                        p = PL[f"lv{half}"]
                        for i in range(4):
                            at = slice(i * 512, (i + 1) * 512)
                            dve.wait_ge(operand_hi, p["O"] + i + 1)
                            V.scalar_tensor_tensor(VL[:, at], PSUM[:, i, :], RT[:, i:i + 1], r32(VH[:, at]), MUL, SUB).then_inc(operand_lo, 1)
                        p = PL[f"latt{half}"]
                        for n in range(16 + 2):
                            pr, qi = divmod(n, 4)
                            new = qi == 0 and n < 16
                            u = p["U"] + n
                            if new:
                                dve.wait_ge(slot_done, p["S"] + pr + 1)
                                for m, (bank, tab_) in enumerate(((7, TAB[:, COSR:COSR + SEQ]), (2 * (u % 2), TAB[:, SINR:SINR + SEQ]),
                                                                  (2 * (u % 2) + 1, R[:, 0:SEQ]))):
                                    V.tensor_tensor(TMP[:, m * TOK:m * TOK + SEQ], PSUM[:, bank, :], tab_, MUL).then_inc(f32_ready, 1)
                                o = p["O"] + 4 * pr
                                dve.wait_ge(f32_ready, p["F"] + 3 * pr + 3)
                                for m in range(2):
                                    lo_of(o + m, win(XL[dst], (5 + m) * TOK, False), TMP[:, m * TOK:m * TOK + SEQ], win(XH[dst], (5 + m) * TOK, False))
                                lo_of(o + 2, win(XL[dst], 7 * TOK, False, slice(0, 64)), TMP[0:64, 2 * TOK:2 * TOK + SEQ], win(XH[dst], 7 * TOK, False, slice(0, 64)))
                                lo_of(o + 3, VL[64:128, 2048:2560], TMP[64:128, 2 * TOK:2 * TOK + SEQ], VH[64:128, 2048:2560])
                                if n >= 1:
                                    att2_tl(u - 1, 512)
                                if n >= 2:
                                    att2_ol(u - 2, src, 4 * half + (n - 2) // 4, (n - 2) % 4)
                                att2_max(u, 0, False)
                                att2_max(u + 1, 1, False)
                                att2_mix(u, 128)
                            else:
                                if n < 16 and qi < 3:
                                    att2_max(u + 1, qi + 1, False)
                                if n < 16:
                                    att2_mix(u, 128 * (qi + 1))
                                if n <= 16:
                                    att2_tl(u - 1, 128 * ((n - 1) % 4 + 1))
                                if n >= 2:
                                    att2_ol(u - 2, src, 4 * half + (n - 2) // 4, (n - 2) % 4)
                    residual_phase("wo3", "mlp2", 8, dst, False)
                    src, dst = dst, src
            norm(PL["end"]["N"] - 1, False, False)
            for c in range(8):
                h = win(H, c * TOK, False)
                V.scalar_tensor_tensor(h, h, gain("final2", c), win(R, 0, False), MUL, MUL).then_inc(out_ready, 1)

        @block.tensor
        def _(pe):
            def three(o, lhs, rhs, first, last):
                TE.matmul(o, lhs[0], rhs[0], start=first, stop=False)
                TE.matmul(o, lhs[0], rhs[1], start=False, stop=False)
                return TE.matmul(o, lhs[1], rhs[0], start=False, stop=last)

            def weight(s, k, n=128):
                return WH[:, s % RS, k * n:(k + 1) * n], WL[:, s % RS, k * n:(k + 1) * n]

            def chunk(x, at, n, rows=slice(0, 128)):
                return XH[x][rows, at:at + n], XL[x][rows, at:at + n]

            def product(s, bank, x, full, w0=0, x0=0, nk=8, operand=None, of=None):
                for k in range(nk):
                    if operand is not None:
                        pe.wait_ge(of or operand_lo, operand + k + 1)
                    w = weight(s, w0 + k)
                    for p in range(3):
                        a = w[1 if p == 2 else 0]
                        for n0, n, b in pieces(full):
                            at = (x0 + k) * TOK + n0
                            ins = TE.matmul(PSUM[:, bank + b, 0:n], a, (XL if p == 1 else XH)[x][:, at:at + n],
                                            start=(k == 0 and p == 0), stop=(k == nk - 1 and p == 2))
                return ins

            def tile(name, j, x, full, nk=8, operand=None, d=0, of=None):
                s, t = PL[name]["S"] + j, PL[name]["T"] + j
                pe.wait_ge(w_lo, s + 1 + d)
                if t - depth(full) + 1 > 0:
                    pe.wait_ge(tile_free, t - depth(full) + 1 + d)
                product(s, tile_bank(t, full), x, full, nk=nk, operand=operand, of=of).then_inc(slot_done, 1)

            def tiles_loop(name, n, x, full, nk=8, operand=None):
                with pe.Fori(0, n // 4) as i:
                    for u in range(4):
                        tile(name, u, x, full, nk, operand if u == 0 else None, i * 4)

            def all_free(name):
                pe.wait_ge(tile_free, PL[name]["T"])

            def norm(n, q, full, by_token):
                pe.wait_ge(sq_added, q)
                for n0, w, b in pieces(full):
                    ins = TE.matmul(PSUM[:, 6 + b, 0:w], ONES, SQA[:, n0:n0 + w], start=True, stop=True)
                if by_token:
                    for i in range(5 if full else 4):
                        t0 = max(0, N_META + 128 * (i - 1)) if full else N_META + 128 * i
                        ins = TE.matmul(PSUM[:, 7, 400 + i:401 + i], SQA[:, t0:t0 + 128], ONES[:, 0:1], start=True, stop=True)
                ins.then_inc(norm_mm, 1)

            def by_tokens(name, nslot, ntile, x, width, kper, t_of, of_k=0, nkk=None):
                p = PL[name]
                total = nslot * kper
                for j in range(nslot):
                    pe.wait_ge(w_lo, p["S"] + j + 1)
                    for kk in range(kper):
                        k = j * kper + kk
                        for i in range(ntile):
                            ins = three(PSUM[:, i, 0:width], chunk(x, (of_k + k) * TOK + t_of(i), 128),
                                        weight(p["S"] + j, kk, width), k == 0, k == total - 1)
                    ins.then_inc(slot_done, 1)

            pe.wait_ge(const_ready, 7)
            src, shared_bank = 0, 0
            for l in range(DEPTH):
                full = l == 0
                dst = 1 - src
                before = PL["load"] if l == 0 else PL[f"down0{len(FF_PARTS) - 1}"]
                all_free(f"glu{l}")
                for j in range(8):
                    tile(f"glu{l}", j, src, True, operand=before["O"] if j == 0 else None)
                    if j == 0:
                        norm(PL[f"glu{l}"]["N"] - 1, before["Q"] + 8, True, True)
                for j in range(8):
                    tile(f"qk{l}", j, src, True)
                all_free(f"v{l}")
                by_tokens(f"v{l}", 4, 5, src, 512, 2, lambda i: max(0, N_META + 128 * (i - 1)))
                pe.wait_ge(operand_lo, PL[f"att{l}"]["O"])
                units, u0 = units1(l), PL[f"att{l}"]["U"]
                for n in range(-1, len(units) + 2):
                    if n + 1 < len(units):
                        u = u0 + n + 1
                        hd, q0, nq, nk = units[n + 1]
                        if u >= 2:
                            pe.wait_ge(probs_ready, u - 1)
                        for c in range(2):
                            rows = slice(64 * c, 64 * c + 64)
                            at = score_at(u, c, nk)
                            cut = (512 if c == 0 else nk - 512) if nk > 512 else nk
                            for k0, k1 in ((0, cut), (cut, nk)):
                                if k1 > k0:
                                    ins = three(PF[:, at + k0:at + k1], chunk(dst, hd * TOK + q0, 128, rows),
                                                chunk(dst, (HEADS + hd) * TOK + k0, k1 - k0, rows), True, True)
                            if c == 0 and nk > 512:
                                shared_bank += 1
                                ins.then_inc(map_done, 1)
                                pe.wait_ge(map_done, shared_bank)
                        ins.then_inc(scores_ready, 1)
                    if n >= 2:
                        hd, q0, nq, nk = units[n - 2]
                        w = u0 + n - 2
                        pe.wait_ge(tl_ready, w + 1)
                        if w >= 1:
                            pe.wait_ge(o_free, w)
                        o_ = PSUM[:, 7, 128 * (w % 2):128 * (w % 2) + nq]
                        nb = (nk - N_META) // 128 if nq == 128 else 0
                        ins = three(o_, (VH[0:N_META, hd * 128:(hd + 1) * 128], VL[0:N_META, hd * 128:(hd + 1) * 128]),
                                    (AH[0:N_META, w % 2, 512:512 + nq], AL[0:N_META, w % 2, 512:512 + nq]), True, nb == 0)
                        for b in range(nb):
                            va = (b + 1) * 512 + hd * 128
                            ins = three(o_, (VH[:, va:va + 128], VL[:, va:va + 128]),
                                        (AH[:, w % 2, 128 * b:128 * (b + 1)], AL[:, w % 2, 128 * b:128 * (b + 1)]), False, b == nb - 1)
                        ins.then_inc(pv_ready, 1)
                    if 1 <= n <= len(units):
                        hd, q0, nq, nk = units[n - 1]
                        v = u0 + n - 1
                        pe.wait_ge(mix_ready, v + 1)
                        if v >= 1:
                            pe.wait_ge(tl_ready, v)
                        if n >= 2:
                            pe.wait_ge(o_free, v)
                        ins = TE.transpose(PSUM[:, 7, 256:256 + nq], PRB[0:nq, v % 2, 0, 0:128], IDENT[0:nq, 0:nq])
                        if nq == 128:
                            for b in range((nk - N_META) // 128):
                                k0 = N_META + 128 * b
                                ins = TE.transpose(PSUM[:, 6, 128 * b:128 * (b + 1)], PRB[:, v % 2, 0, k0:k0 + 128], IDENT)
                        ins.then_inc(tr_ready, 1)
                p = PL[f"post{l}"]
                for e in range(4):
                    pe.wait_ge(stat_sq, p["W"] + e + 1)
                    for n0, w, b in pieces(full):
                        ins = TE.matmul(PSUM[:, 2 * e + b, 0:w], ONES, TMP[:, e * TOK + n0:e * TOK + n0 + w], start=True, stop=True)
                    ins.then_inc(stat_mm, 1)
                pe.wait_ge(stat_std, p["A"] + 1)
                pe.wait_ge(conv_done, (l + 1) * DVE_TAPS)
                pe.wait_ge(tap_added, (l + 1) * KW)
                for c in range(4):
                    for n0, w, b in pieces(full):
                        ins = TE.matmul(PSUM[:, b, 0:w], ONES, Z[:, c, KW - 1 + n0:KW - 1 + n0 + w], start=(c == 0), stop=(c == 3))
                ins.then_inc(stat_mm, 1)
                pe.wait_ge(stat_std, p["A"] + 2)
                for c in range(4):
                    pe.wait_ge(stat_sq, p["W"] + 4 + c + 1)
                    for n0, w, b in pieces(full):
                        ins = TE.matmul(PSUM[:, 2 + b, 0:w], ONES, PRBF[:, c * TOK + n0:c * TOK + n0 + w], start=(c == 0), stop=(c == 3))
                    ins.then_inc(stat_mm, 1)
                pe.wait_ge(stat_std, p["A"] + 6)
                for j in range(8):
                    tile(f"wo{l}", j, src, full, operand=p["O"] if j == 0 else None)
                o0 = PL[f"wo{l}"]["O"]
                for p_, f in enumerate(FF_PARTS):
                    if p_ == 0:
                        tile(f"up{l}0", 0, dst, full, operand=o0)
                        norm(PL[f"wo{l}"]["N"], PL[f"wo{l}"]["Q"] + 8, full, False)
                        for u in range(1, 4):
                            tile(f"up{l}0", u, dst, full)
                        with pe.Fori(1, f // 2) as i:
                            for u in range(4):
                                tile(f"up{l}0", u, dst, full, d=i * 4)
                    else:
                        tiles_loop(f"up{l}{p_}", 2 * f, dst, full)
                    tiles_loop(f"down{l}{p_}", 8, src, full, f, PL[f"up{l}{p_}"]["O"])
                src = dst
            norm(PL["x2"]["N"] - 1, PL["x2"]["Q"], False, False)
            dst = 1 - src
            for j in range(5):
                tile("qi", j, src, False, operand=PL["x2"]["O"] if j == 0 else None)
                if j == 0:
                    norm(PL["qi"]["N"] - 1, PL["x2"]["Q"] + 8, False, True)
            pe.wait_ge(wi_lo, 1)
            for i in range(4):
                for k in range(8):
                    ins = three(PSUM[:, 5, i * 8:(i + 1) * 8], chunk(src, k * TOK + N_META + 128 * i, 128),
                                (WIH[:, k * 8:(k + 1) * 8], WIL[:, k * 8:(k + 1) * 8]), k == 0, k == 7)
            ins.then_inc(wi_mm, 1)
            pe.wait_ge(operand_lo, PL["q2"]["O"])
            pe.wait_ge(r_ready, PL["qi"]["N"])
            g0 = 0
            for i in range(1, 4):
                for hh in range(IDX_HEADS):
                    rows = slice(64 * (hh % 2), 64 * (hh % 2) + 64)
                    nk = 128 * (i + 1)
                    if g0 >= 2:
                        pe.wait_ge(idx_relu, g0 - 1)
                    three(PSUM[:, 6 + g0 % 2, 0:nk], chunk(dst, (hh // 2) * TOK + N_META + 128 * i, 128, rows),
                          (VH[rows, 2048:2048 + nk], VL[rows, 2048:2048 + nk]), True, True).then_inc(idx_scores, 1)
                    g0 += 1
            for j in range(10):
                tile("q2", j, src, False)
            all_free("v2")
            by_tokens("v2", 2, 4, src, 256, 4, lambda i: N_META + 128 * i)
            pe.wait_ge(operand_lo, PL["att2"]["O"])

            def att2_scores(u, qi, qpair, kpair):
                pe.wait_ge(probs_ready, u - 1)
                for c in range(2):
                    ins = three(PSUM[:, 2 * (u % 2) + c, 0:128 * (qi + 1)], qpair(c), kpair(c), True, True)
                ins.then_inc(scores_ready, 1)

            def att2_transpose(v, qi):
                pe.wait_ge(mix_ready, v + 1)
                pe.wait_ge(tl_ready, v)
                for c in range(2):
                    for b in range(qi + 1):
                        ins = TE.transpose(PSUM[:, 4 + c, 128 * b:128 * (b + 1)], PRB[:, v % 2, c, 128 * b:128 * (b + 1)], IDENT)
                ins.then_inc(tr_ready, 1)

            def att2_values(w, qi, vat):
                pe.wait_ge(tl_ready, w + 1)
                pe.wait_ge(o_free, w)
                o_ = PSUM[:, 6, 256 * (w % 2):256 * (w % 2) + 256].rearrange("p (c n) -> p c n", c=2)
                for b in range(qi + 1):
                    a_ = vat(b)
                    pr_ = [x_[:, w % 2, :].rearrange("p (c n) -> p c n", c=2)[:, :, 128 * b:128 * (b + 1)] for x_ in (AH, AL)]
                    ins = three(o_, (VH[:, a_:a_ + 128], VL[:, a_:a_ + 128]), pr_, b == 0, b == qi)
                ins.then_inc(pv_ready, 1)

            u0 = PL["att2"]["U"]
            for n in range(-1, PAIRS * 4 + 2):
                u = u0 + n
                if n + 1 < PAIRS * 4:
                    qi, t = divmod(n + 1, PAIRS)
                    att2_scores(u + 1, qi, lambda c: chunk(dst, t * TOK + N_META + 128 * qi, 128, slice(64 * c, 64 * c + 64)),
                                lambda c: tuple(b[64 * c:64 * c + 64, 1024 + (t // 4) * 512:1024 + (t // 4) * 512 + 128 * (qi + 1)] for b in (VH, VL)))
                if 1 <= n <= PAIRS * 4:
                    att2_transpose(u - 1, (n - 1) // PAIRS)
                if n >= 2:
                    qi, t = divmod(n - 2, PAIRS)
                    att2_values(u - 2, qi, lambda b: b * 256 + (t // 4) * 128)
            pe.wait_ge(o_free, u0 + PAIRS * 4)
            for j in range(8):
                tile("wo2", j, src, False)
            src, dst = dst, src
            for l in range(DEPTH):
                before = PL["wo2"] if l == 0 else PL["wo3"]
                for p_ in range(FF2_PARTS):
                    if p_ == 0:
                        tile(f"mup{l}0", 0, src, False, operand=before["O"])
                        norm(before["N"], before["Q"] + 8, False, False)
                        for u in range(1, 4):
                            tile(f"mup{l}0", u, src, False)
                        for u in range(4):
                            tile(f"mup{l}0", 4 + u, src, False)
                    else:
                        tiles_loop(f"mup{l}{p_}", 8, src, False)
                    tiles_loop(f"mdown{l}{p_}", 8, dst, False, 8, PL[f"mup{l}{p_}"]["O"])
                if l == 0:
                    o0 = PL[f"mdown0{FF2_PARTS - 1}"]
                    for j in range(7):
                        tile("lat", j, src, False, operand=o0["O"] if j == 0 else None)
                        if j == 0:
                            norm(o0["N"], o0["Q"] + 8, False, False)
                    p = PL["lat"]
                    pe.wait_ge(stat_sq, p["W"] + 5)
                    pe.wait_ge(r_ready, p["N"])
                    sq = [ORAW[:, j * SEQ:(j + 1) * SEQ] for j in range(4)] + [CACC[:, 0, 0:SEQ]]
                    for j in range(5):
                        TE.matmul(PSUM[:, 6 if j < 3 else 7, :], ONES, sq[j], start=j in (0, 3), stop=j in (2, 4))
                    for i in range(4):
                        for j in (3, 4):
                            ins = TE.matmul(PSUM[:, 5, i:i + 1], sq[j][:, 128 * i:128 * (i + 1)], ONES[:, 0:1], start=j == 3, stop=j == 4)
                    ins.then_inc(stat_mm, 1)
                    for half in range(2):
                        if half == 0:
                            pe.wait_ge(operand_lo, p["O"] + 7)
                            all_free("lv0")
                        else:
                            pe.wait_ge(o_free, PL["lv1"]["U"])
                        for k in range(2):
                            s = PL[f"lv{half}"]["S"] + k
                            pe.wait_ge(w_lo, s + 1)
                            for i in range(4):
                                ins = three(PSUM[:, i, :], chunk(dst, (3 + k) * TOK + N_META + 128 * i, 128), weight(s, 0, 512), k == 0, k == 1)
                            ins.then_inc(slot_done, 1)
                        pe.wait_ge(lat_ready, 1)
                        pp = PL[f"latt{half}"]

                        def scores(u, qi):
                            att2_scores(u, qi, lambda c: chunk(dst, (5 + c) * TOK + N_META + 128 * qi, 128),
                                        lambda c: chunk(dst, 7 * TOK + N_META, 128 * (qi + 1)) if c == 0 else tuple(b[:, 2048:2048 + 128 * (qi + 1)] for b in (VH, VL)))

                        for n in range(16 + 2):
                            pr, qi = divmod(n, 4)
                            u = pp["U"] + n
                            new = qi == 0 and n < 16
                            if new:
                                s = pp["S"] + pr
                                pe.wait_ge(w_lo, s + 1)
                                pe.wait_ge(probs_ready, u)
                                pe.wait_ge(operand_lo, pp["O"] + 4 * pr)
                                product(s, 7, dst, False, 0, 0, 3)
                                product(s, 2 * (u % 2), dst, False, 3, 0, 3)
                                product(s, 2 * (u % 2) + 1, dst, False, 6, 3, 2).then_inc(slot_done, 1)
                                if n >= 1:
                                    att2_transpose(u - 1, 3)
                                if n >= 2:
                                    att2_values(u - 2, 2, lambda b: b * 512 + ((n - 2) // 4) * 128)
                                pe.wait_ge(operand_lo, pp["O"] + 4 * pr + 4)
                                scores(u, 0)
                                scores(u + 1, 1)
                            else:
                                if n < 16 and qi < 3:
                                    scores(u + 1, qi + 1)
                                if n <= 16:
                                    att2_transpose(u - 1, (n - 1) % 4)
                                if n >= 2:
                                    att2_values(u - 2, (n - 2) % 4, lambda b: b * 512 + ((n - 2) // 4) * 128)
                    pe.wait_ge(o_free, PL["wo3"]["U"])
                    for j in range(8):
                        tile("wo3", j, src, False)
                    src, dst = dst, src
            norm(PL["end"]["N"] - 1, PL["end"]["Q"], False, False)


def _slot(w):
    k, n = w.shape[0] // 128, w.shape[1]
    s = np.zeros((128, SLOT), np.float32)
    s[:, :k * n] = w.reshape(k, 128, n).transpose(1, 0, 2).reshape(128, k * n)
    return s


def _tiles(w, cols=None):
    n = w.shape[1] // 128 if cols is None else len(cols)
    return [_slot(w[:, j * 128:(j + 1) * 128] if cols is None else w[:, cols[j]]) for j in range(n)]


ROT_ROWS = np.array([*range(0, 8), *range(16, 40), *range(8, 16), *range(40, 64)])


def _pair_heads(t):
    base = 8 * (t // 4)
    return base + t % 4, base + 4 + t % 4


def _weight_stream(i):
    s = []
    cat = np.concatenate
    for l in range(DEPTH):
        w = i["w_in"][l]
        for c in range(4):
            s += _tiles(w[:, 2048 + 128 * c:2176 + 128 * c]) + _tiles(w[:, 1536 + 128 * c:1664 + 128 * c])
        s += _tiles(w[:, 0:1024])
        s += [_slot(w[256 * j:256 * (j + 1), 1024:1536]) for j in range(4)]
        s += _tiles(i["w_out"][l])
        f0 = 0
        gu, dn = i["w_gate_up"][l], i["w_down"][l]
        for f in FF_PARTS:
            for c in range(f0, f0 + f):
                s += _tiles(gu[:, 128 * c:128 * (c + 1)]) + _tiles(gu[:, FF * 128 + 128 * c:FF * 128 + 128 * (c + 1)])
            s += _tiles(dn[128 * f0:128 * (f0 + f)])
            f0 += f
    w = i["a_w_in_2"][0]
    s += _tiles(w, [cat([1536 + 64 * (2 * t + b) + ROT_ROWS for b in range(2)]) for t in range(4)] + [cat([2048 + ROT_ROWS] * 2)])
    s += _tiles(w, [cat([64 * h + ROT_ROWS for h in _pair_heads(t)]) for t in range(8)])
    s += _tiles(w, [cat([1024 + 64 * (2 * j + b) + ROT_ROWS for b in range(2)]) for j in range(2)])
    s += [_slot(w[512 * j:512 * (j + 1), 1280:1536]) for j in range(2)]
    s += _tiles(i["a_w_out_2"][0][cat([64 * h + np.arange(64) for t in range(8) for h in _pair_heads(t)])])
    for l in range(DEPTH):
        up, dn = i["mlp_w_up_2"][l], i["mlp_w_down_2"][l]
        for p in range(FF2_PARTS):
            s += _tiles(up[:, 1024 * p:1024 * (p + 1)])
            s += _tiles(dn[1024 * p:1024 * (p + 1)])
        if l == 0:
            w = i["b_w_in_2"][0]
            swap = np.array([*range(16, 32), *range(0, 16)])
            s += _tiles(w[:, 0:640]) + _tiles(w, [cat([640 + np.arange(32)] * 4), cat([640 + swap] * 4)])
            kv, qu = i["b_w_kv_up_2"][0], i["b_w_q_up_2"][0]
            for half in range(2):
                cols = cat([128 * h + 64 + np.arange(64) for h in range(8 * half, 8 * half + 8)])
                s += [_slot(kv[128 * k:128 * (k + 1)][:, cols]) for k in range(2)]
                for t in range(4 * half, 4 * half + 4):
                    a, b = 96 * 2 * t, 96 * (2 * t + 1)
                    nope, rope, sw = np.arange(64), 64 + np.arange(32), 64 + swap
                    qa = qu[:, a + cat([nope, rope, sw])].reshape(3, 128, 128)
                    qb = qu[:, b + cat([rope, sw, nope])].reshape(3, 128, 128)
                    kn = kv[:, cat([128 * 2 * t + nope, 128 * (2 * t + 1) + nope])].reshape(2, 128, 128)
                    s.append(_slot(cat([qa, qb, kn]).reshape(1024, 128)))
            s += _tiles(i["b_w_out_2"][0])
    assert len(s) == NSLOT, (len(s), NSLOT)
    return np.stack(s)


def _columns(v):
    return np.ascontiguousarray(np.asarray(v).reshape(-1, 128).T)


def _shape_constants():
    p = np.arange(128)
    inv = (10000.0 ** (-np.arange(0, 64, 2, dtype=np.float32) / np.float32(64))).astype(np.float32)
    ang = (inv[p % 32][:, None] * np.arange(TOK, dtype=np.float32)[None, :]).astype(np.float32)
    sgn = np.where(p % 64 < 32, -1.0, 1.0)[:, None]
    tab = np.concatenate([np.cos(ang.astype(np.float64)), np.sin(ang.astype(np.float64)) * sgn], 1).astype(np.float32)
    q, k = np.meshgrid(p, p, indexing="ij")
    masks = np.concatenate([np.where(k <= q, 0.0, NEG), np.where(k // 64 <= q // 64, 0.0, NEG)], 1).astype(np.float32)
    inva = (500000.0 ** (-np.arange(0, 16, 2, dtype=np.float32) / np.float32(16))).astype(np.float32)
    r = p % 32
    ca = np.where(r < 8, inva[np.minimum(r, 7)], 0).astype(np.float32)
    sa = np.where(p % 64 < 32, -1.0, 1.0).astype(np.float32)
    invb = (500000.0 ** (-np.arange(0, 32, 2, dtype=np.float32) / np.float32(32))).astype(np.float32)
    cb = invb[p % 16]
    sb_ = np.where(p % 32 < 16, -1.0, 1.0).astype(np.float32)
    return tab, masks, np.stack([ca, sa, cb, sb_], 1)


def kernel(**inputs):
    import concourse.bacc as bacc
    from concourse import mybir
    from concourse.bass_utils import run_bass_kernel_spmd

    i = {k: np.asarray(v) for k, v in inputs.items()}
    tab1, masks, rows = _shape_constants()
    xT = np.concatenate([i["meta_tokens"], i["x"][0]], 0).T
    params = np.concatenate([
        _columns(i["norm1_g"]), _columns(i["norm2_g"]), _columns(i["final_g"]), _columns(i["attn_norm_2"]),
        _columns(i["mlp_norm_2"]), _columns(i["final_norm_2"]), _columns(i["b_glu"]),
        i["conv_w"].reshape(DEPTH, KW, CC, 128).transpose(3, 0, 2, 1).reshape(128, -1),
        _columns(i["conv_b"]), _columns(i["conv_ln_g"]), _columns(i["conv_ln_b"]), _columns(i["subln_g"]),
        _columns(i["b_q_norm_2"]), _columns(i["b_kv_norm_2"]), rows], 1)
    lamv = np.stack([i["lam_q1"], i["lam_k1"], i["lam_q2"], i["lam_k2"]], 1).reshape(1, 512)
    wiw = i["a_w_in_2"][0][:, 2112:2120].reshape(8, 128, 8).transpose(1, 0, 2).reshape(128, 64)
    arrays = dict(wstream=_weight_stream(i), xT=xT, params=params, lamv=lamv, tab1=tab1, masks=masks, wiw=wiw,
                  pos=i["positions_2"].astype(np.int32))
    nc = bacc.Bacc("TRN2", target_bir_lowering=False, num_devices=1, dynamic_dma_scratch_size=1024)
    arrays = {k: np.ascontiguousarray(v) for k, v in arrays.items()}
    aps = [nc.dram_tensor(k + "_dram", v.shape, mybir.dt.from_np(v.dtype), kind="ExternalInput").ap() for k, v in arrays.items()]
    outT = nc.dram_tensor("outT", (D, SEQ), mybir.dt.float32, kind="ExternalOutput").ap()
    build(nc, *aps, outT)
    r = run_bass_kernel_spmd(nc, [{k + "_dram": v for k, v in arrays.items()}], core_ids=[0])
    return np.ascontiguousarray(r.results[0]["outT"].T)[None]
```
